# Optimizing a Trainium2 kernel written in Bass

```python
import jax, jax.numpy as jnp
from jax import lax
import numpy as np
import math
import jax
import jax.numpy as jnp

D_MODEL = 1024
BATCH = 1
SEQ = 256
DEPTH = 2

N_EVEN = (DEPTH + 1) // 2
N_ODD = DEPTH // 2
D_FF = 2816
NORM_EPS = 1e-6

ATTN_HEADS = 8
HEAD_DIM = 64
ATTN_WIDTH = ATTN_HEADS * HEAD_DIM
ROT_DIM = HEAD_DIM // 4
ROPE_THETA = 500000.0
MOBA_BLOCK = 256
MOBA_TOPK = 3
MOBA_Q_CHUNK = 32

LRU_WIDTH = 512
LRU_HEADS = 8
LRU_HEAD_DIM = LRU_WIDTH // LRU_HEADS
LRU_CONV = 4
LRU_C = 8.0

AB_IN = 3 * ATTN_WIDTH + 2 * LRU_WIDTH
AB_OUT = ATTN_WIDTH + LRU_WIDTH

SC_WIDTH = D_MODEL
SC_CONV = 3


def rms_norm(x, g):
    xf = x.astype(jnp.float32)
    y = xf * lax.rsqrt(jnp.mean(xf * xf, axis=-1, keepdims=True) + NORM_EPS) * g.astype(jnp.float32)
    return y.astype(x.dtype)

def swiglu(h, w_gate, w_up, w_down):
    return (jax.nn.silu(h @ w_gate) * (h @ w_up)) @ w_down

def causal_depthwise_conv(x, w):
    k, c = w.shape
    return lax.conv_general_dilated(
        x, w[:, None, :].astype(x.dtype), window_strides=(1,), padding=[(k - 1, 0)],
        dimension_numbers=("NWC", "WIO", "NWC"), feature_group_count=c)

def partial_rope(x, pos):
    half = ROT_DIM // 2
    inv_freq = ROPE_THETA ** (-jnp.arange(0, ROT_DIM, 2, dtype=jnp.float32) / ROT_DIM)
    ang = pos[:, None] * inv_freq[None, :]
    cos = jnp.cos(ang)[None, :, None, :]
    sin = jnp.sin(ang)[None, :, None, :]
    xf = x.astype(jnp.float32)
    x1, x2, rest = xf[..., :half], xf[..., half:ROT_DIM], xf[..., ROT_DIM:]
    out = jnp.concatenate([x1 * cos - x2 * sin, x2 * cos + x1 * sin, rest], axis=-1)
    return out.astype(x.dtype)

def moba_attention(q, k, v):
    b, s, h, hd = q.shape
    n_blk = -(-s // MOBA_BLOCK)
    sp = n_blk * MOBA_BLOCK
    pad = ((0, 0), (0, sp - s), (0, 0), (0, 0))
    qt = jnp.pad(q, pad).transpose(0, 2, 1, 3)
    kt = jnp.pad(k, pad).transpose(0, 2, 1, 3)
    vt = jnp.pad(v, pad).transpose(0, 2, 1, 3)
    kb = kt.reshape(b, h, n_blk, MOBA_BLOCK, hd)
    vb = vt.reshape(b, h, n_blk, MOBA_BLOCK, hd)
    kmean = jnp.mean(kb.astype(jnp.float32), axis=3)
    n_sel = min(MOBA_TOPK, n_blk - 1)
    scale = hd ** -0.5
    blk_ids = jnp.arange(n_blk)
    bi = jnp.arange(b)[:, None, None]
    hi = jnp.arange(h)[None, :, None]
    neg = jnp.float32(-1e30)

    def chunk(c):
        start = c * MOBA_Q_CHUNK
        own = start // MOBA_BLOCK
        qc = lax.dynamic_slice_in_dim(qt, start, MOBA_Q_CHUNK, axis=2)
        qpos = start + jnp.arange(MOBA_Q_CHUNK)
        k_own = lax.dynamic_index_in_dim(kb, own, axis=2, keepdims=False)
        v_own = lax.dynamic_index_in_dim(vb, own, axis=2, keepdims=False)
        kpos = own * MOBA_BLOCK + jnp.arange(MOBA_BLOCK)
        s_own = jnp.einsum("bhqd,bhkd->bhqk", qc, k_own).astype(jnp.float32) * scale
        s_own = jnp.where(kpos[None, :] <= qpos[:, None], s_own, neg)
        logits = [s_own]
        vals = [v_own]
        if n_sel > 0:
            g = jnp.einsum("bhqd,bhnd->bhqn", qc.astype(jnp.float32), kmean)
            g = jnp.where(blk_ids < own, g, neg)
            _, idx = lax.top_k(g, n_sel)
            valid = idx < own
            for j in range(n_sel):
                ks = kb[bi, hi, idx[..., j]]
                vs = vb[bi, hi, idx[..., j]]
                sj = jnp.einsum("bhqd,bhqkd->bhqk", qc, ks).astype(jnp.float32) * scale
                logits.append(jnp.where(valid[..., j][..., None], sj, neg))
                vals.append(vs)
        p = jax.nn.softmax(jnp.concatenate(logits, axis=-1), axis=-1)
        p = p.astype(v.dtype)
        out = jnp.einsum("bhqk,bhkd->bhqd", p[..., :MOBA_BLOCK], vals[0])
        for j in range(1, n_sel + 1):
            pj = p[..., j * MOBA_BLOCK:(j + 1) * MOBA_BLOCK]
            out = out + jnp.einsum("bhqk,bhqkd->bhqd", pj, vals[j])
        return out

    outs = lax.map(chunk, jnp.arange(sp // MOBA_Q_CHUNK))
    outs = outs.transpose(1, 0, 3, 2, 4).reshape(b, sp, h, hd)[:, :s]
    return outs.reshape(b, s, h * hd)

def rg_lru(xc, wa, ba, wx, bx, lam):
    b, s, w = xc.shape
    xf = xc.astype(jnp.float32).reshape(b, s, LRU_HEADS, LRU_HEAD_DIM)
    r = jax.nn.sigmoid(jnp.einsum("bshi,hij->bshj", xf, wa.astype(jnp.float32)) + ba.astype(jnp.float32))
    i = jax.nn.sigmoid(jnp.einsum("bshi,hij->bshj", xf, wx.astype(jnp.float32)) + bx.astype(jnp.float32))
    log_a = -LRU_C * r * jax.nn.softplus(-lam.astype(jnp.float32)).reshape(LRU_HEADS, LRU_HEAD_DIM)
    a = jnp.exp(log_a)
    u = jnp.sqrt(-jnp.expm1(2.0 * log_a)) * (i * xf)
    a = a.reshape(b, s, w)
    u = u.reshape(b, s, w)

    def combine(e1, e2):
        a1, u1 = e1
        a2, u2 = e2
        return a1 * a2, a2 * u1 + u2

    _, hseq = lax.associative_scan(combine, (a, u), axis=1)
    return hseq.astype(xc.dtype)

def first_inputs(seed: int = 0) -> dict:
    key = jax.random.key(seed)
    ks = jax.random.split(key, 24)
    f32 = jnp.float32

    def nrm(k, shape, fan_in):
        return jax.random.normal(k, shape, f32) * (fan_in ** -0.5)

    x = jax.random.normal(ks[0], (BATCH, SEQ, D_MODEL), f32)
    ffn1_w_gate = nrm(ks[1], (DEPTH, D_MODEL, D_FF), D_MODEL)
    ffn1_w_up = nrm(ks[2], (DEPTH, D_MODEL, D_FF), D_MODEL)
    ffn1_w_down = nrm(ks[3], (DEPTH, D_FF, D_MODEL), D_FF)
    ffn2_w_gate = nrm(ks[4], (DEPTH, D_MODEL, D_FF), D_MODEL)
    ffn2_w_up = nrm(ks[5], (DEPTH, D_MODEL, D_FF), D_MODEL)
    ffn2_w_down = nrm(ks[6], (DEPTH, D_FF, D_MODEL), D_FF)
    norm_pre = 1.0 + 0.05 * jax.random.normal(ks[7], (DEPTH, 3, D_MODEL), f32)
    norm_post = 1.0 + 0.05 * jax.random.normal(ks[8], (DEPTH, 3, D_MODEL), f32)
    ab_w_in = nrm(ks[9], (N_EVEN, D_MODEL, AB_IN), D_MODEL)
    ab_w_out = nrm(ks[10], (N_EVEN, AB_OUT, D_MODEL), AB_OUT)
    lru_conv_w = nrm(ks[11], (N_EVEN, LRU_CONV, LRU_WIDTH), LRU_CONV)
    lru_conv_b = 0.01 * jax.random.normal(ks[12], (N_EVEN, LRU_WIDTH), f32)
    lru_gate_a_w = nrm(ks[13], (N_EVEN, LRU_HEADS, LRU_HEAD_DIM, LRU_HEAD_DIM), LRU_HEAD_DIM)
    lru_gate_a_b = 0.01 * jax.random.normal(ks[14], (N_EVEN, LRU_HEADS, LRU_HEAD_DIM), f32)
    lru_gate_x_w = nrm(ks[15], (N_EVEN, LRU_HEADS, LRU_HEAD_DIM, LRU_HEAD_DIM), LRU_HEAD_DIM)
    lru_gate_x_b = 0.01 * jax.random.normal(ks[16], (N_EVEN, LRU_HEADS, LRU_HEAD_DIM), f32)
    a_c = jax.random.uniform(ks[17], (N_EVEN, LRU_WIDTH), f32, 0.9, 0.999)
    a0 = a_c ** (1.0 / LRU_C)
    lru_lambda = jnp.log(a0) - jnp.log1p(-a0)
    c_w_in = nrm(ks[18], (N_ODD, D_MODEL, 3 * SC_WIDTH), D_MODEL)
    c_conv_w = nrm(ks[19], (N_ODD, SC_CONV, SC_WIDTH), SC_CONV)
    c_w_out = nrm(ks[20], (N_ODD, SC_WIDTH, D_MODEL), SC_WIDTH)
    return {
        "x": x,
        "ffn1_w_gate": ffn1_w_gate, "ffn1_w_up": ffn1_w_up, "ffn1_w_down": ffn1_w_down,
        "ffn2_w_gate": ffn2_w_gate, "ffn2_w_up": ffn2_w_up, "ffn2_w_down": ffn2_w_down,
        "norm_pre": norm_pre, "norm_post": norm_post,
        "ab_w_in": ab_w_in, "ab_w_out": ab_w_out,
        "lru_conv_w": lru_conv_w, "lru_conv_b": lru_conv_b,
        "lru_gate_a_w": lru_gate_a_w, "lru_gate_a_b": lru_gate_a_b,
        "lru_gate_x_w": lru_gate_x_w, "lru_gate_x_b": lru_gate_x_b,
        "lru_lambda": lru_lambda,
        "c_w_in": c_w_in, "c_conv_w": c_conv_w, "c_w_out": c_w_out,
    }

def first_block(x, ffn1_w_gate, ffn1_w_up, ffn1_w_down, ffn2_w_gate, ffn2_w_up, ffn2_w_down,
              norm_pre, norm_post, ab_w_in, ab_w_out, lru_conv_w, lru_conv_b,
              lru_gate_a_w, lru_gate_a_b, lru_gate_x_w, lru_gate_x_b, lru_lambda,
              c_w_in, c_conv_w, c_w_out):
    b, s, d = x.shape
    pos = jnp.arange(s, dtype=jnp.float32)
    for l in range(DEPTH):
        hdn = swiglu(rms_norm(x, norm_pre[l, 0]), ffn1_w_gate[l], ffn1_w_up[l], ffn1_w_down[l])
        x = x + 0.5 * rms_norm(hdn, norm_post[l, 0])

        h = rms_norm(x, norm_pre[l, 1])
        if l % 2 == 0:
            e = l // 2
            p = h @ ab_w_in[e]
            q = p[..., :ATTN_WIDTH].reshape(b, s, ATTN_HEADS, HEAD_DIM)
            k = p[..., ATTN_WIDTH:2 * ATTN_WIDTH].reshape(b, s, ATTN_HEADS, HEAD_DIM)
            v = p[..., 2 * ATTN_WIDTH:3 * ATTN_WIDTH].reshape(b, s, ATTN_HEADS, HEAD_DIM)
            lru_x = p[..., 3 * ATTN_WIDTH:3 * ATTN_WIDTH + LRU_WIDTH]
            lru_g = p[..., 3 * ATTN_WIDTH + LRU_WIDTH:]
            attn = moba_attention(partial_rope(q, pos), partial_rope(k, pos), v)
            xc = causal_depthwise_conv(lru_x, lru_conv_w[e]) + lru_conv_b[e]
            rec = rg_lru(xc, lru_gate_a_w[e], lru_gate_a_b[e], lru_gate_x_w[e], lru_gate_x_b[e],
                         lru_lambda[e]) * jax.nn.gelu(lru_g)
            mix = jnp.concatenate([attn, rec], axis=-1) @ ab_w_out[e]
        else:
            o = l // 2
            p = h @ c_w_in[o]
            gate_b = p[..., :SC_WIDTH]
            gate_c = p[..., SC_WIDTH:2 * SC_WIDTH]
            xt = p[..., 2 * SC_WIDTH:]
            mix = (gate_b * causal_depthwise_conv(gate_c * xt, c_conv_w[o])) @ c_w_out[o]
        x = x + rms_norm(mix, norm_post[l, 1])

        hdn = swiglu(rms_norm(x, norm_pre[l, 2]), ffn2_w_gate[l], ffn2_w_up[l], ffn2_w_down[l])
        x = x + 0.5 * rms_norm(hdn, norm_post[l, 2])
    return x


D_MIX = D_MODEL
S5_WIDTH = D_MIX // 2
S5_GROUP_CH = 16
S5_GROUPS = S5_WIDTH // S5_GROUP_CH
S5_STATE = 64
S5_CHUNK = 128
GLA_WIDTH = D_MIX - S5_WIDTH
GLA_HEADS = 4
GLA_DK = GLA_WIDTH // 2
GLA_HEAD_K = GLA_DK // GLA_HEADS
GLA_HEAD_V = GLA_WIDTH // GLA_HEADS
GLA_GATE_RANK = 16
GLA_GATE_TAU = 16.0
GLA_CHUNK = 64
IN_SPLITS = (S5_WIDTH, S5_WIDTH + GLA_DK, S5_WIDTH + 2 * GLA_DK, S5_WIDTH + 2 * GLA_DK + GLA_WIDTH, S5_WIDTH + 2 * GLA_DK + 2 * GLA_WIDTH)
IN_COLS = S5_WIDTH + 2 * GLA_DK + 2 * GLA_WIDTH + GLA_GATE_RANK
D_FF_2 = 7 * D_MODEL // 2
N_EXPERTS = 8
TOP_K = 2
N_DENSE = (DEPTH + 1) // 2
N_MOE = DEPTH // 2
DN_ALPHA = (2.0 * DEPTH) ** 0.25
DN_BETA = (8.0 * DEPTH) ** -0.25
N_MOD = 6
MOD_STD = 0.1
LN_EPS = 1e-5
RMS_EPS = 1e-6


def _layer_norm(x, gain, bias):
    xf = x.astype(jnp.float32)
    mu = jnp.mean(xf, axis=-1, keepdims=True)
    var = jnp.mean(jnp.square(xf - mu), axis=-1, keepdims=True)
    return ((xf - mu) * lax.rsqrt(var + LN_EPS)).astype(x.dtype) * gain + bias

def _rms_norm(x, gain):
    xf = x.astype(jnp.float32)
    return xf * lax.rsqrt(jnp.mean(xf * xf, axis=-1, keepdims=True) + RMS_EPS) * gain.astype(jnp.float32)

def _linear_recurrence_op(e1, e2):
    a1, b1 = e1
    a2, b2 = e2
    return a1 * a2, a2 * b1 + b2

def _s5_group(u, lam_re, lam_im, log_dt, b_re, b_im, c_re, c_im, d_skip, w_glu, b_glu):
    bsz, seq, _ = u.shape
    n_chunks = seq // S5_CHUNK
    f32 = jnp.float32
    uf = u.astype(f32)
    lam = lax.complex(lam_re.astype(f32), lam_im.astype(f32))
    dt = jnp.exp(log_dt.astype(f32))[:, None]
    lam_bar = jnp.exp(lam * dt)
    b_mat = lax.complex(b_re.astype(f32), b_im.astype(f32))
    b_bar = ((lam_bar - 1.0) / lam)[:, :, None] * b_mat
    c_mat = lax.complex(c_re.astype(f32), c_im.astype(f32))
    u_chunks = uf.reshape(bsz, n_chunks, S5_CHUNK, S5_GROUPS, S5_GROUP_CH).transpose(1, 0, 2, 3, 4)
    a_elems = jnp.broadcast_to(lam_bar, (bsz, S5_CHUNK, S5_GROUPS, S5_STATE))

    def chunk_step(h, u_c):
        bu = jnp.einsum('gph,blgh->blgp', b_bar, u_c.astype(jnp.complex64))
        a_cum, s = lax.associative_scan(_linear_recurrence_op, (a_elems, bu), axis=1)
        states = s + a_cum * h[:, None]
        y = jnp.einsum('ghp,blgp->blgh', c_mat, states).real
        return states[:, -1], y

    h0 = jnp.zeros((bsz, S5_GROUPS, S5_STATE), jnp.complex64)
    _, y = lax.scan(chunk_step, h0, u_chunks)
    y = y.transpose(1, 0, 2, 3, 4).reshape(bsz, seq, S5_WIDTH) + d_skip.astype(f32) * uf
    y = jax.nn.gelu(y).astype(u.dtype)
    return y * jax.nn.sigmoid(y @ w_glu + b_glu)

def _gla_group(q, k, v, g_out, a_low, w_alpha_up, b_alpha, head_gain):
    bsz, seq, _ = q.shape
    nc = seq // GLA_CHUNK
    f32 = jnp.float32

    def heads(t, dh):
        return t.astype(f32).reshape(bsz, nc, GLA_CHUNK, GLA_HEADS, dh).transpose(1, 0, 3, 2, 4)

    log_alpha = jax.nn.log_sigmoid((a_low @ w_alpha_up + b_alpha).astype(f32)) / GLA_GATE_TAU
    qc = heads(q, GLA_HEAD_K) * (GLA_HEAD_K ** -0.5)
    kc = heads(k, GLA_HEAD_K)
    vc = heads(v, GLA_HEAD_V)
    bc = jnp.cumsum(heads(log_alpha, GLA_HEAD_K), axis=3)
    causal = jnp.tril(jnp.ones((GLA_CHUNK, GLA_CHUNK), dtype=bool))

    def chunk_step(state, inp):
        q_c, k_c, v_c, b_c = inp
        o_inter = jnp.einsum('bhik,bhkv->bhiv', q_c * jnp.exp(b_c), state)
        diff = b_c[:, :, :, None, :] - b_c[:, :, None, :, :]
        decay = jnp.exp(jnp.where(causal[:, :, None], diff, -jnp.inf))
        scores = jnp.einsum('bhik,bhjk,bhijk->bhij', q_c, k_c, decay)
        o_intra = jnp.einsum('bhij,bhjv->bhiv', scores, v_c)
        b_last = b_c[:, :, -1:, :]
        k_dec = k_c * jnp.exp(b_last - b_c)
        new_state = jnp.exp(b_last[:, :, 0, :])[..., None] * state + jnp.einsum('bhjk,bhjv->bhkv', k_dec, v_c)
        return new_state, o_inter + o_intra

    s0 = jnp.zeros((bsz, GLA_HEADS, GLA_HEAD_K, GLA_HEAD_V), f32)
    _, o = lax.scan(chunk_step, s0, (qc, kc, vc, bc))
    o = o.transpose(1, 0, 3, 2, 4).reshape(bsz, seq, GLA_HEADS, GLA_HEAD_V)
    o = _rms_norm(o, head_gain.reshape(GLA_HEADS, GLA_HEAD_V)).reshape(bsz, seq, GLA_WIDTH)
    return (o * jax.nn.silu(g_out.astype(f32))).astype(q.dtype)

def _swiglu(x, w_gate, w_up, w_down):
    return (jax.nn.silu(x @ w_gate) * (x @ w_up)) @ w_down

def _moe_swiglu(x, w_router, b_router, w_gate, w_up, w_down):
    logits = (x @ w_router).astype(jnp.float32) + b_router.astype(jnp.float32)
    top_vals, top_idx = lax.top_k(logits, TOP_K)
    top_w = jax.nn.softmax(top_vals, axis=-1)
    combine = jnp.sum(jax.nn.one_hot(top_idx, N_EXPERTS, dtype=jnp.float32) * top_w[..., None], axis=-2)
    out = jnp.zeros_like(x)
    for e in range(N_EXPERTS):
        out = out + combine[..., e:e + 1].astype(x.dtype) * _swiglu(x, w_gate[e], w_up[e], w_down[e])
    return out

def second_inputs(seed: int = 0) -> dict:
    key = jax.random.key(seed)
    ks = jax.random.split(key, 32)
    f32 = jnp.float32

    def nrm(k, shape, std):
        return std * jax.random.normal(k, shape, f32)

    G, P, H = S5_GROUPS, S5_STATE, S5_GROUP_CH
    return {
        'x': jax.random.normal(ks[0], (BATCH, SEQ, D_MODEL), f32),
        'c': jax.random.normal(ks[1], (BATCH, D_MODEL), f32),
        'mod_w': nrm(ks[2], (DEPTH, D_MODEL, N_MOD * D_MODEL), MOD_STD * D_MODEL ** -0.5),
        'mod_b': nrm(ks[3], (DEPTH, N_MOD * D_MODEL), 0.01),
        'w_in': nrm(ks[4], (DEPTH, D_MODEL, IN_COLS), D_MODEL ** -0.5),
        'w_out': nrm(ks[5], (DEPTH, D_MIX, D_MODEL), DN_BETA * D_MIX ** -0.5),
        's5_lam_re': -0.5 * jnp.exp(nrm(ks[6], (DEPTH, G, P), 0.05)),
        's5_lam_im': math.pi * jnp.arange(P, dtype=f32)[None, None, :] + nrm(ks[7], (DEPTH, G, P), 0.01),
        's5_log_dt': jax.random.uniform(ks[8], (DEPTH, G), f32, math.log(1e-3), math.log(1e-1)),
        's5_b_re': nrm(ks[9], (DEPTH, G, P, H), (2.0 * H) ** -0.5),
        's5_b_im': nrm(ks[10], (DEPTH, G, P, H), (2.0 * H) ** -0.5),
        's5_c_re': nrm(ks[11], (DEPTH, G, H, P), (2.0 * P) ** -0.5),
        's5_c_im': nrm(ks[12], (DEPTH, G, H, P), (2.0 * P) ** -0.5),
        's5_d': nrm(ks[13], (DEPTH, S5_WIDTH), 1.0),
        's5_w_glu': nrm(ks[14], (DEPTH, S5_WIDTH, S5_WIDTH), S5_WIDTH ** -0.5),
        's5_b_glu': nrm(ks[15], (DEPTH, S5_WIDTH), 0.01),
        'gla_w_alpha_up': nrm(ks[16], (DEPTH, GLA_GATE_RANK, GLA_DK), GLA_GATE_RANK ** -0.5),
        'gla_b_alpha': nrm(ks[17], (DEPTH, GLA_DK), 0.01),
        'gla_head_gain': 1.0 + nrm(ks[18], (DEPTH, GLA_WIDTH), 0.02),
        'ln_mix_g': 1.0 + nrm(ks[19], (DEPTH, D_MODEL), 0.02),
        'ln_mix_b': nrm(ks[20], (DEPTH, D_MODEL), 0.01),
        'ffn_w_gate': nrm(ks[21], (N_DENSE, D_MODEL, D_FF_2), D_MODEL ** -0.5),
        'ffn_w_up': nrm(ks[22], (N_DENSE, D_MODEL, D_FF_2), D_MODEL ** -0.5),
        'ffn_w_down': nrm(ks[23], (N_DENSE, D_FF_2, D_MODEL), DN_BETA * D_FF_2 ** -0.5),
        'moe_w_router': nrm(ks[24], (N_MOE, D_MODEL, N_EXPERTS), D_MODEL ** -0.5),
        'moe_b_router': nrm(ks[25], (N_MOE, N_EXPERTS), 0.01),
        'moe_w_gate': nrm(ks[26], (N_MOE, N_EXPERTS, D_MODEL, D_FF_2), D_MODEL ** -0.5),
        'moe_w_up': nrm(ks[27], (N_MOE, N_EXPERTS, D_MODEL, D_FF_2), D_MODEL ** -0.5),
        'moe_w_down': nrm(ks[28], (N_MOE, N_EXPERTS, D_FF_2, D_MODEL), DN_BETA * D_FF_2 ** -0.5),
        'ln_ffn_g': 1.0 + nrm(ks[29], (DEPTH, D_MODEL), 0.02),
        'ln_ffn_b': nrm(ks[30], (DEPTH, D_MODEL), 0.01),
    }

def second_block(x, c, mod_w, mod_b, w_in, w_out, s5_lam_re, s5_lam_im, s5_log_dt, s5_b_re, s5_b_im, s5_c_re, s5_c_im, s5_d, s5_w_glu, s5_b_glu, gla_w_alpha_up, gla_b_alpha, gla_head_gain, ln_mix_g, ln_mix_b, ffn_w_gate, ffn_w_up, ffn_w_down, moe_w_router, moe_b_router, moe_w_gate, moe_w_up, moe_w_down, ln_ffn_g, ln_ffn_b):
    c_act = jax.nn.silu(c)
    for layer in range(DEPTH):
        mod = c_act @ mod_w[layer] + mod_b[layer]
        sh_m, sc_m, gt_m, sh_f, sc_f, gt_f = jnp.split(mod[:, None, :], N_MOD, axis=-1)
        h = x * (1 + sc_m) + sh_m
        u, q, k, v, g_out, a_low = jnp.split(h @ w_in[layer], IN_SPLITS, axis=-1)
        y_s5 = _s5_group(u, s5_lam_re[layer], s5_lam_im[layer], s5_log_dt[layer], s5_b_re[layer], s5_b_im[layer], s5_c_re[layer], s5_c_im[layer], s5_d[layer], s5_w_glu[layer], s5_b_glu[layer])
        y_gla = _gla_group(q, k, v, g_out, a_low, gla_w_alpha_up[layer], gla_b_alpha[layer], gla_head_gain[layer])
        y = jnp.concatenate([y_s5, y_gla], axis=-1) @ w_out[layer]
        x = _layer_norm(DN_ALPHA * x + (1 + gt_m) * y, ln_mix_g[layer], ln_mix_b[layer])
        h = x * (1 + sc_f) + sh_f
        i = layer // 2
        if layer % 2 == 0:
            f = _swiglu(h, ffn_w_gate[i], ffn_w_up[i], ffn_w_down[i])
        else:
            f = _moe_swiglu(h, moe_w_router[i], moe_b_router[i], moe_w_gate[i], moe_w_up[i], moe_w_down[i])
        x = _layer_norm(DN_ALPHA * x + (1 + gt_f) * f, ln_ffn_g[layer], ln_ffn_b[layer])
    return x


def setup_inputs(seed=0):
    out = dict(first_inputs(seed))
    for name, value in second_inputs(seed + 1).items():
        if name != "x":
            out[name + "_2"] = value
    return out


def reference(
    x, ffn1_w_gate, ffn1_w_up, ffn1_w_down, ffn2_w_gate, ffn2_w_up, ffn2_w_down, norm_pre,
    norm_post, ab_w_in, ab_w_out, lru_conv_w, lru_conv_b, lru_gate_a_w, lru_gate_a_b,
    lru_gate_x_w, lru_gate_x_b, lru_lambda, c_w_in, c_conv_w, c_w_out, c_2, mod_w_2, mod_b_2,
    w_in_2, w_out_2, s5_lam_re_2, s5_lam_im_2, s5_log_dt_2, s5_b_re_2, s5_b_im_2, s5_c_re_2,
    s5_c_im_2, s5_d_2, s5_w_glu_2, s5_b_glu_2, gla_w_alpha_up_2, gla_b_alpha_2, gla_head_gain_2,
    ln_mix_g_2, ln_mix_b_2, ffn_w_gate_2, ffn_w_up_2, ffn_w_down_2, moe_w_router_2,
    moe_b_router_2, moe_w_gate_2, moe_w_up_2, moe_w_down_2, ln_ffn_g_2, ln_ffn_b_2,
):
    x = first_block(
        x, ffn1_w_gate, ffn1_w_up, ffn1_w_down, ffn2_w_gate, ffn2_w_up, ffn2_w_down, norm_pre,
        norm_post, ab_w_in, ab_w_out, lru_conv_w, lru_conv_b, lru_gate_a_w, lru_gate_a_b,
        lru_gate_x_w, lru_gate_x_b, lru_lambda, c_w_in, c_conv_w, c_w_out,
    )
    return second_block(
        x, c_2, mod_w_2, mod_b_2, w_in_2, w_out_2, s5_lam_re_2, s5_lam_im_2, s5_log_dt_2,
        s5_b_re_2, s5_b_im_2, s5_c_re_2, s5_c_im_2, s5_d_2, s5_w_glu_2, s5_b_glu_2,
        gla_w_alpha_up_2, gla_b_alpha_2, gla_head_gain_2, ln_mix_g_2, ln_mix_b_2, ffn_w_gate_2,
        ffn_w_up_2, ffn_w_down_2, moe_w_router_2, moe_b_router_2, moe_w_gate_2, moe_w_up_2,
        moe_w_down_2, ln_ffn_g_2, ln_ffn_b_2,
    )


_drawn_inputs = setup_inputs


def setup_inputs(seed=0):
    import zlib

    import numpy as np

    out = dict(_drawn_inputs(seed))
    spreads = {}
    factors = {'lru_gate_a_b': 7.186,
     'lru_gate_x_b': 7.593,
     'mod_b_2': 3.749,
     's5_lam_re_2': 64.0,
     's5_lam_im_2': 29.344,
     's5_log_dt_2': 32.472,
     's5_b_re_2': 33.512,
     's5_b_im_2': 43.824,
     's5_c_re_2': 46.816,
     's5_c_im_2': 40.544,
     's5_b_glu_2': 51.32,
     'gla_b_alpha_2': 8.0,
     'gla_head_gain_2': 5.431,
     'moe_b_router_2': 4.804,
     'ln_ffn_b_2': 3.464}
    for name, (base, spread) in spreads.items():
        noise = np.random.default_rng([zlib.crc32(name.encode()), seed]).standard_normal(out[name].shape)
        drawn = base * np.exp(spread * noise) if base else spread * noise
        out[name] = jnp.asarray(drawn.astype(out[name].dtype))
    for name, factor in factors.items():
        out[name] = (out[name] * factor).astype(out[name].dtype)
    return out
```

```python
from contextlib import ExitStack

import numpy as np

import concourse.bass as bass
from concourse import mybir

F32 = mybir.dt.float32
F32R = mybir.dt.float32r
I32 = mybir.dt.int32
ALU = mybir.AluOpType
ACT = mybir.ActivationFunctionType
AX = mybir.AxisListType

P = 128
S = 256
NT = S // P
D = 1024
KD = D // P
FF1, FF2 = 2816, 3584
NF1, NF2 = FF1 // P, FF2 // P
HD = 64
NH = 8
NE = 8
BLK = 1024
EPS = 1e-6
LN_EPS = 1e-5
ALPHA = 4.0 ** 0.25
LRU_C = 8.0
TWO_PI = (6.28125, 0.0019350051879882812, 3.0199159819567e-07)
LEVELS = (64, 32, 16, 8, 4, 2, 1)

SUBS = [("ffn", NF1), ("ab", 10), ("ffn", NF1), ("ffn", NF1), ("c", 11), ("ffn", NF1),
        ("mix2", 10), ("ffn", NF2), ("mix2", 10), ("moe", NE * NF2)]
START = [0]
for _, n in SUBS:
    START.append(START[-1] + n)
NU = START[-1] + 1
FSTART = [0]
for kind, n in SUBS:
    FSTART.append(FSTART[-1] + (n if kind in ("ffn", "moe") else 0))

COLS = {}
_at = 0
for name, n in [("c", KD), ("norm_pre", 6 * KD), ("conv_w", 16), ("conv_b", 4), ("ga_b", 4),
                ("gx_b", 4), ("lam", 4), ("c_conv", 3 * KD), ("mod_b", 96), ("s5_d", 8),
                ("glu_b", 8), ("alpha_b", 4), ("re", 32), ("im", 32), ("ldt", 32)]:
    COLS[name] = (_at, n)
    _at += n
NCOL = _at

CONST = {}
_at = 0
for name, n in [("ident", P), ("amask", 3 * P), ("cos", S), ("sin", S), ("rot", P),
                ("lmask", len(LEVELS) * P)]:
    CONST[name] = (_at, n)
    _at += n
NCONST = _at


class Chain:

    def __init__(self, eng, sem):
        self.eng, self.sem, self.n, self.reg = eng, sem, 0, 0

    def link(self, ins):
        self.n += 1
        ins.then_inc(self.sem, 1)
        self.eng.wait_ge(self.sem, self.reg + self.n)


def ge(eng, sm, n, dyn=0):
    if not isinstance(dyn, int):
        eng.wait_ge(sm, dyn + n)
    elif n + dyn > 0:
        eng.wait_ge(sm, n + dyn)


def program(nc, A, out):
    with ExitStack() as ctx:
        def sb(name, shape, dt=F32):
            return ctx.enter_context(nc.sbuf_tensor(name, shape, dt))

        def sem(name):
            return ctx.enter_context(nc.semaphore(name))

        raw_gu = [sb(f"raw_gu{i}", [P, 2 * BLK]) for i in range(2)]
        raw_d = [sb(f"raw_d{i}", [P, BLK]) for i in range(2)]
        wh_gu = [sb(f"wh_gu{i}", [P, 2, KD, P], F32R) for i in range(2)]
        wl_gu = [sb(f"wl_gu{i}", [P, 2, KD, P], F32R) for i in range(2)]
        wh_d = [sb(f"wh_d{i}", [P, BLK], F32R) for i in range(2)]
        wl_d = [sb(f"wl_d{i}", [P, BLK], F32R) for i in range(2)]
        X = sb("residual", [P, NT, D])
        XH, XL = sb("xT_hi", [P, KD, S], F32R), sb("xT_lo", [P, KD, S], F32R)
        MH, ML = sb("mixT_hi", [P, KD, S], F32R), sb("mixT_lo", [P, KD, S], F32R)
        ROW = sb("rows", [P, 3 * D])
        cst = sb("const", [P, NCONST])
        col = sb("cols", [P, NCOL])
        HH = [sb(f"h_hi{i}", [P, S], F32R) for i in range(2)]
        HL = [sb(f"h_lo{i}", [P, S], F32R) for i in range(2)]
        modT = sb("modT", [P, 96])
        small = sb("small", [P, 256])
        s5p = sb("s5p", [P, 27, 32])
        s5i = sb("s5i", [P, 32], I32)
        wau = sb("w_alpha", [16, S])
        RW = sb("router_w", [P, KD, NE])
        scr = sb("scratch", [P, 16384])
        PA = ctx.enter_context(nc.psum_tensor("acc", [P, 4, 512], F32))
        PB = ctx.enter_context(nc.psum_tensor("work", [P, 4, 512], F32))

        def C(name, i=0, n=1):
            return col[:, COLS[name][0] + i:COLS[name][0] + i + n]

        def K(name):
            return cst[:, CONST[name][0]:CONST[name][0] + CONST[name][1]]

        ident = K("ident")
        ones, eps_rms, eps_ln = (small[:, i:i + 1] for i in range(3))
        ss, rs, mu, nmu = (small[:, 8 + 2 * i:10 + 2 * i] for i in range(4))
        lru_k, lru_t = small[:, 16:20], [small[:, 20 + 4 * i:24 + 4 * i] for i in range(5)]
        c_act = small[:, 40:48]
        smax, nmax, ssum, srec = (small[:, 48 + 4 * i:52 + 4 * i] for i in range(4))
        gss, grs = small[:, 64:72], small[:, 72:80]
        rt = [small[:, 80 + 16 * i:96 + 16 * i].rearrange("p (t e) -> p t e", t=NT) for i in range(8)]
        rt1 = [small[:, 208 + 2 * i:210 + 2 * i] for i in range(6)]

        def view(at, n):
            return scr[:, at:at + n]

        XN = view(0, 2048).rearrange("p (t d) -> p t d", t=NT)
        XTF = view(2048, 2048).rearrange("p (k s) -> p k s", k=KD)
        TMP = view(2048, 2048).rearrange("p (t d) -> p t d", t=NT)
        SG = [view(4096 + 256 * i, 256) for i in range(2)]
        HF = [view(4608 + 256 * i, 256) for i in range(2)]
        ACC = view(5120, 2048).rearrange("p (t d) -> p t d", t=NT)
        JUNK = view(7168, 1024)
        E = view(8192, 8192).rearrange("p (c t s) -> p c t s", c=2, t=16)
        ET = view(5120, 2048)
        MACC = view(0, 3072)
        MW = [view(12288 + 1024 * i, 1024) for i in range(3)]
        QK = view(0, 2048).rearrange("p (k s) -> p k s", k=8)
        LX = view(2048, 1040).rearrange("p (k s) -> p k s", k=4)
        LG, VA = view(3088, 1024), view(4112, 1024).rearrange("p (t d) -> p t d", t=NT)
        PR = [view(5136 + 384 * i, 384) for i in range(2)]
        PT = [view(5904 + 384 * i, 384) for i in range(2)]
        XC, RR, II, AA, TH, UU = (view(6672 + 1024 * i, 1024) for i in range(6))
        ROT = view(12816, 2048).rearrange("p (k s) -> p k s", k=8)
        LGW = ROW[:, 1024:2048].rearrange("p (g t m) -> p g t m", g=2, t=4)
        CXT = [view(256 * i, 256) for i in range(2)]
        CM = [view(512 + 258 * i, 258) for i in range(2)]
        CY = [view(1100 + 256 * i, 256) for i in range(2)]
        UT = view(0, 1024).rearrange("p (k s) -> p k s", k=4)
        QG, KG = view(1024, 512), view(1536, 512)
        AL = view(2048, 256)
        VG = view(2304, 1024).rearrange("p (t d) -> p t d", t=NT)
        GO = view(3328, 1024).rearrange("p (t d) -> p t d", t=NT)
        BT, DF, QS, KS = (view(4352 + 512 * i, 512) for i in range(4))
        MT = view(6400, 1024)
        LT = view(7424, 512)
        GJ = view(7936, 128)
        SC = ROW[:, 0:1536].rearrange("p (w h i) -> p w h i", w=3, h=4)
        OG = ROW[:, 1536:2560].rearrange("p (t d) -> p t d", t=NT)
        HG = ROW[:, 2560:3072]
        SBM = [view(1024 + 512 * i, 512).rearrange("p (c t m) -> p c t m", c=2, t=2) for i in range(2)]
        W = view(2048, 1024).rearrange("p (c t s) -> p c t s", c=2, t=2)
        PP = [view(3072 + 512 * i, 512) for i in range(4)]
        YT = view(5120, 1024).rearrange("p (k s) -> p k s", k=4)
        CRAW = view(6144, 1024).rearrange("p (c t h) -> p c t h", c=2, t=16)
        CS = ROW[:, 0:1536].rearrange("p (c t h) -> p c t h", c=3, t=16)
        GL = view(2048, 1024).rearrange("p (k s) -> p k s", k=4)

        cols_in, consts_in, x_in, router_in = (sem(n) for n in ("cols_in", "consts_in", "x_in", "router_in"))
        gain_in, lruw_in, ln_in, headgain_in, alphaw_in = (
            sem(n) for n in ("gain_in", "lruw_in", "ln_in", "headgain_in", "alphaw_in"))
        s5b_in, s5c_in = [sem(f"s5b_in{i}") for i in range(2)], sem("s5c_in")
        gu_landed = [sem(f"gu_landed{i}") for i in range(2)]
        d_landed = [sem(f"d_landed{i}") for i in range(2)]
        gu_hi, d_hi, gu_lo, d_lo = sem("gu_hi"), sem("d_hi"), sem("gu_lo"), sem("d_lo")
        gu_used, d_used = sem("gu_used"), sem("d_used")
        dve_step, pool_step = sem("dve_step"), sem("pool_step")
        small_ready, c_act_done = sem("small_ready"), sem("c_act_done")
        par_exp, par_angle, par_trig, par_ready = (sem("par_" + n) for n in ("exp", "angle", "trig", "ready"))
        mod_in = [sem(f"mod_in{i}") for i in range(3)]
        mod_term, mod_sums, mod_cols, mod_copied = (sem("mod_" + n) for n in ("term", "sums", "cols", "copied"))
        silu_done, h_ready = sem("silu_done"), sem("h_ready")
        sq_done, root_done, x_done, mean_done = (sem(n) for n in ("sq_done", "root_done", "x_done", "mean_done"))
        xn_done, xt_ps, xt_f, xt_h, xt_l = (sem(n) for n in ("xn_done", "xt_ps", "xt_f", "xt_h", "xt_l"))
        t_evac = sem("t_evac")
        mix_h, mix_l = sem("mix_h"), sem("mix_l")
        gt_ps = sem("gt_ps")
        a = {n: sem("ab_" + n) for n in (
            "v_sb", "rot", "roped", "scores", "masked", "nmax", "exp", "probs", "pT", "pT_sb", "av",
            "conv", "gates", "sig", "la", "ea", "neg", "root", "rec", "gelu")}
        c_x, c_y = sem("c_x_copied"), sem("c_y")
        g = {n: sem("gla_" + n) for n in (
            "vg_sb", "z", "zabs", "zexp", "diff", "exp", "qks", "scores", "masked", "o", "sq",
            "root", "gout", "og", "oT")}
        s = {n: sem("s5_" + n) for n in (
            "table", "c_ready", "bu", "bu_used", "prod", "y", "ysum", "gelu", "yh", "yl", "sig", "gated")}
        logits, route_d, route_e, moe_acc, out_done = (
            sem(n) for n in ("logits", "route_d", "route_e", "moe_acc", "out_done"))

        T_OF = {"ab": 16, "mix2": 9}
        TSTART = [0]
        for kind, _ in SUBS:
            TSTART.append(TSTART[-1] + T_OF.get(kind, 0))
        MIXES = {"ab": 5, "c": 8, "mix2": 3}
        MSTART = [0]
        for kind, _ in SUBS:
            MSTART.append(MSTART[-1] + MIXES.get(kind, 0))
        MOD_AT = [0, 2, 3, 7]
        MOD_START = [START[b] for b in MOD_AT]
        SECOND = 6

        def tile2(x):
            return x.rearrange("p a b -> p (a b)")

        def c_bank(n, i):
            return (PA if n % 2 else PB)[:, i, 0:S]

        block = ctx.enter_context(nc.Block())

        @block.sync
        def _(sp):
            sp.dma_start(col[:, :], A["cols"]).then_inc(cols_in, 16)
            sp.dma_start(cst[:, :], A["consts"]).then_inc(consts_in, 16)

            def load(n, dyn=0):
                k = n % 2
                ge(sp, gu_lo, n - 1, dyn)
                sp.dma_start(raw_gu[k][:, :], A["w_gu"][dyn + n]).then_inc(gu_landed[k], 16)
                ge(sp, d_lo, n - 1, dyn)
                sp.dma_start(raw_d[k][:, :], A["w_d"][dyn + n]).then_inc(d_landed[k], 16)

            sp.dma_start(X[:, :, :], A["x"].rearrange("(t p) d -> p t d", p=P)).then_inc(x_in, 16)
            load(0)
            load(1)
            with sp.Fori(0, (NU - 2) // 2) as j:
                load(2, j * 2)
                load(3, j * 2)
            if NU % 2:
                load(NU - 1)
            sp.wait_ge(x_done, len(SUBS))
            sp.dma_start(out.rearrange("(t p) d -> p t d", p=P), X[:, :, :]).then_inc(out_done, 16)
            sp.wait_ge(out_done, 16)

        @block.scalar
        def _(act):
            def hi_gu(n, dyn=0):
                k = n % 2
                act.wait_ge(gu_landed[k], dyn * 8 + 16 * (n // 2 + 1))
                ge(act, gu_used, n - 1, dyn)
                act.activation(wh_gu[k][:, :, :, :].rearrange("p a k n -> p (a k n)"), raw_gu[k][:, :],
                               ACT.Copy).then_inc(gu_hi, 1)

            def hi_d(n, dyn=0):
                k = n % 2
                act.wait_ge(d_landed[k], dyn * 8 + 16 * (n // 2 + 1))
                ge(act, d_used, n - 1, dyn)
                act.activation(wh_d[k][:, :], raw_d[k][:, :], ACT.Copy).then_inc(d_hi, 1)

            def hi(n, dyn=0):
                hi_gu(n, dyn)
                hi_d(n, dyn)

            sums = [0]

            def squares(t, src, bias=None):
                ge(act, sq_done, sums[0])
                act.activation(JUNK, src, ACT.Square, accum_out=ss[:, t:t + 1],
                               **({} if bias is None else {"bias": bias})).then_inc(sq_done, 1)
                sums[0] += 1

            def root(eps):
                act.wait_ge(sq_done, sums[0])
                act.activation(rs, ss, ACT.Sqrt, bias=eps, scale=1.0 / D).then_inc(root_done, 1)

            def pre(b):
                if b < SECOND:
                    if b == 0:
                        act.wait_ge(x_in, 16)
                        act.wait_ge(small_ready, 1)
                    else:
                        act.wait_ge(x_done, b)
                    for t in range(NT):
                        squares(t, X[:, t, :])
                    root(eps_rms)
                for j in range(4):
                    act.wait_ge(xt_f, 4 * b + j + 1)
                    act.activation(XH[:, 2 * j:2 * j + 2, :], XTF[:, 2 * j:2 * j + 2, :], ACT.Copy).then_inc(xt_h, 1)

            def post(b):
                if b < SECOND:
                    act.wait_ge(d_used, START[b + 1])
                    for t in range(NT):
                        squares(t, tile2(PA[:, 2 * t:2 * t + 2, :]))
                    root(eps_rms)
                else:
                    act.wait_ge(mean_done, b - SECOND + 1)
                    for t in range(NT):
                        squares(t, TMP[:, t, :], nmu[:, t:t + 1])
                    root(eps_ln)

            def ffn(n0, dyn, nf):
                def steps(at):
                    for n in (n0, n0 + 1):
                        hi_gu(n + 1, at)
                        ge(act, gu_used, n + 1, at)
                        act.activation(SG[n % 2], PB[:, n % 2, 0:S], ACT.Silu).then_inc(silu_done, 1)
                        hi_d(n + 1, at)

                if n0 == 0:
                    steps(0)
                with act.Fori(1 if n0 == 0 else 0, nf // 2) as j:
                    steps(dyn + j * 2)

            def mix_hi(dst, src):
                act.activation(dst, src, ACT.Copy).then_inc(mix_h, 1)

            def ab(b):
                U = START[b]
                for u in range(7):
                    hi(U + u + 1)
                for h in range(NH):
                    act.wait_ge(a["nmax"], h + 1)
                    for q, (at, n) in enumerate(((0, P), (P, S))):
                        m = 2 * (h % 2) + q
                        act.activation(PR[h % 2][:, at:at + n], PR[h % 2][:, at:at + n], ACT.Exp,
                                       bias=nmax[:, m:m + 1], accum_out=ssum[:, m:m + 1]).then_inc(a["exp"], 1)
                    act.wait_ge(a["pT"], h + 1)
                    act.activation(PT[h % 2], PA[:, 2 + h % 2, 0:3 * P], ACT.Copy).then_inc(a["pT_sb"], 1)
                    if h % 2:
                        act.wait_ge(a["av"], h + 1)
                        mix_hi(MH[:, h // 2, :], PB[:, 2 + (h // 2) % 2, 0:S])
                for gate, (dst, bias) in enumerate(((RR, "ga_b"), (II, "gx_b"))):
                    for t in range(4):
                        act.wait_ge(a["gates"], 4 * gate + t + 1)
                        ps = (PB if gate == 0 else PA)[:, t, 0:S]
                        act.activation(dst[:, t * S:(t + 1) * S], ps, ACT.Sigmoid, bias=C(bias, t)).then_inc(a["sig"], 1)
                act.wait_ge(a["la"], 1)
                act.activation(AA, RR, ACT.Exp).then_inc(a["ea"], 1)
                act.activation(TH, RR, ACT.Tanh).then_inc(a["ea"], 1)
                act.wait_ge(a["neg"], 1)
                act.activation(UU, TH, ACT.Sqrt, scale=-1.0).then_inc(a["root"], 1)
                act.activation(LG, LG, ACT.Gelu_apprx_tanh).then_inc(a["gelu"], 1)
                act.wait_ge(a["rec"], 1)
                mix_hi(MH[:, 4:8, :], UU.rearrange("p (k s) -> p k s", k=4))
                for u in range(7, 10):
                    hi(U + u + 1)

            def cmix(b):
                U = START[b]
                for n in range(8):
                    hi(U + n + 1)
                    act.wait_ge(d_used, U + n + 1)
                    act.activation(CXT[n % 2], c_bank(n, 2), ACT.Copy).then_inc(c_x, 1)
                    act.wait_ge(c_y, n + 1)
                    mix_hi(MH[:, n, :], CY[n % 2])
                for u in range(8, 11):
                    hi(U + u + 1)

            def mix2(b):
                U, n = START[b], (b - SECOND) // 2
                for u in range(6):
                    hi(U + u + 1)
                act.wait_ge(g["zabs"], n + 1)
                act.activation(LT, LT, ACT.Exp, scale=-1.0).then_inc(g["zexp"], 1)
                act.wait_ge(g["zexp"], 2 * n + 1)
                act.activation(LT, LT, ACT.Ln, bias=ones).then_inc(g["zexp"], 1)
                for j in range(8):
                    act.wait_ge(g["diff"], 2 * (8 * n + j + 1))
                    act.activation(DF, DF, ACT.Exp, scale=1.0 / 16.0).then_inc(g["exp"], 1)
                act.wait_ge(g["o"], n + 1)
                for t in range(NT):
                    for h in range(4):
                        ge(act, g["sq"], 8 * n + 4 * t + h)
                        act.activation(GJ, PB[:, t, h * P:(h + 1) * P], ACT.Square,
                                       accum_out=gss[:, 4 * t + h:4 * t + h + 1]).then_inc(g["sq"], 1)
                act.wait_ge(g["sq"], 8 * (n + 1))
                act.activation(grs, gss, ACT.Sqrt, bias=eps_rms, scale=1.0 / P).then_inc(g["root"], 1)
                act.activation(GO, GO, ACT.Silu).then_inc(g["gout"], 1)
                for t in range(NT):
                    act.wait_ge(g["oT"], 2 * n + t + 1)
                    mix_hi(MH[:, 4:8, t * P:(t + 1) * P], PB[:, 2 + t, :].rearrange("p (k s) -> p k s", k=4))
                act.wait_ge(s["ysum"], 4 * (n + 1))
                act.activation(YT, YT, ACT.Gelu_apprx_tanh).then_inc(s["gelu"], 1)
                act.wait_ge(s["gelu"], n + 1)
                act.activation(XH[:, 0:4, :], YT, ACT.Copy).then_inc(s["yh"], 1)
                hi(U + 7)
                for t in range(4):
                    act.wait_ge(gu_used if t < 2 else d_used, U + 7)
                    act.activation(GL[:, t, :], PB[:, t, 0:S], ACT.Sigmoid, bias=C("glu_b", 4 * n + t)).then_inc(s["sig"], 1)
                act.wait_ge(s["gated"], n + 1)
                mix_hi(MH[:, 0:4, :], GL)
                for u in range(7, 10):
                    hi(U + u + 1)

            def moe(b):
                act.wait_ge(route_d, 1)
                act.activation(rt1[3], rt1[2], ACT.Exp).then_inc(route_e, 1)
                with act.Fori(0, NE) as e:
                    ffn(START[b], e * NF2, NF2)

            act.wait_ge(cols_in, 16)
            act.activation(c_act, C("c", 0, KD), ACT.Silu).then_inc(c_act_done, 1)
            act.activation(s5p[:, 0, :], C("ldt", 0, 32), ACT.Exp).then_inc(par_exp, 1)
            act.activation(lru_t[0], C("lam", 0, 4), ACT.Exp, scale=-1.0).then_inc(par_exp, 1)
            act.wait_ge(par_angle, 1)
            act.activation(s5p[:, 8, :], s5p[:, 1, :], ACT.Exp).then_inc(par_trig, 1)
            act.activation(s5p[:, 9, :], s5p[:, 1, :], ACT.Tanh, scale=0.5).then_inc(par_trig, 1)
            act.activation(s5p[:, 10, :], s5p[:, 5, :], ACT.Sin).then_inc(par_trig, 1)
            act.activation(s5p[:, 11, :], s5p[:, 6, :], ACT.Sin).then_inc(par_trig, 1)
            act.activation(s5p[:, 12, :], s5p[:, 5, :], ACT.Sin, scale=0.5).then_inc(par_trig, 1)
            act.activation(lru_t[2], lru_t[1], ACT.Ln).then_inc(par_trig, 1)
            hi(0)
            for b, (kind, nf) in enumerate(SUBS):
                pre(b)
                if kind == "ffn":
                    ffn(START[b], 0, nf)
                elif kind == "ab":
                    ab(b)
                elif kind == "c":
                    cmix(b)
                elif kind == "mix2":
                    mix2(b)
                else:
                    moe(b)
                post(b)

        @block.vector
        def _(dve):
            chain = Chain(dve, dve_step)
            link = chain.link
            TT, TS, STT = dve.tensor_tensor, dve.tensor_scalar, dve.scalar_tensor_tensor

            def lo_gu(n, dyn=0):
                k = n % 2
                ge(dve, gu_hi, n + 1, dyn)
                wh, wl = (w[k][:, :, :, :].rearrange("p a k n -> p (a k n)") for w in (wh_gu, wl_gu))
                TT(wl, raw_gu[k][:, :], wh.bitcast(F32), ALU.subtract).then_inc(gu_lo, 1)

            def lo_d(n, dyn=0):
                k = n % 2
                ge(dve, d_hi, n + 1, dyn)
                TT(wl_d[k][:, :], raw_d[k][:, :], wh_d[k][:, :].bitcast(F32), ALU.subtract).then_inc(d_lo, 1)

            def lo(n, dyn=0):
                lo_gu(n, dyn)
                lo_d(n, dyn)

            def parameters():
                dve.memset(ones, 1.0)
                dve.memset(eps_rms, EPS)
                dve.memset(eps_ln, LN_EPS).then_inc(small_ready, 1)
                dve.wait_ge(cols_in, 16)

                def q(i):
                    return s5p[:, i, :]
                re, im = C("re", 0, 32), C("im", 0, 32)
                dve.wait_ge(par_exp, 2)
                TT(q(1), re, q(0), ALU.mult)
                link(TT(q(2), im, q(0), ALU.mult))
                link(TS(s5i[:, :], q(2), 1.0 / (2 * np.pi), None, ALU.mult))
                link(dve.tensor_copy(q(3), s5i[:, :]))
                link(STT(q(4), q(3), -TWO_PI[0], q(2), ALU.mult, ALU.add))
                link(STT(q(4), q(3), -TWO_PI[1], q(4), ALU.mult, ALU.add))
                link(STT(q(4), q(3), -TWO_PI[2], q(4), ALU.mult, ALU.add))
                link(TS(q(5), q(4), 3.1415925, -3.1415925, ALU.min, ALU.max))
                link(STT(q(7), q(5), -1.0, q(5), ALU.mult, ALU.max))
                link(TS(lru_t[1], lru_t[0], 1.0, None, ALU.add))
                TS(q(6), q(7), -1.0, float(np.pi / 2), ALU.mult, ALU.add).then_inc(par_angle, 1)
                dve.wait_ge(par_trig, 6)
                link(STT(q(13), q(8), 1.0, q(9), ALU.add, ALU.mult))
                link(TS(q(14), q(13), 1.0, None, ALU.add))
                TT(q(15), q(13), q(11), ALU.mult)
                link(TT(q(16), q(12), q(12), ALU.mult))
                link(STT(q(17), q(16), -2.0, q(15), ALU.mult, ALU.add))
                link(TT(q(18), q(14), q(10), ALU.mult))
                TT(q(19), re, re, ALU.mult)
                link(TT(q(20), im, im, ALU.mult))
                link(TT(q(19), q(19), q(20), ALU.add))
                link(dve.reciprocal(q(20), q(19)))
                TT(q(21), q(17), re, ALU.mult)
                TT(q(22), q(18), im, ALU.mult)
                TT(q(23), q(18), re, ALU.mult)
                link(TT(q(24), q(17), im, ALU.mult))
                link(TT(q(21), q(21), q(22), ALU.add))
                link(TT(q(23), q(23), q(24), ALU.subtract))
                link(TT(q(25), q(21), q(20), ALU.mult))
                link(TT(q(26), q(23), q(20), ALU.mult))
                e_, w_, ln_, one_, d_ = lru_t
                link(TS(d_, w_, -1.0, None, ALU.add))
                link(TS(one_, d_, 0.0, None, ALU.is_equal))
                link(TT(d_, d_, one_, ALU.add))
                link(dve.reciprocal(d_, d_))
                link(TT(ln_, ln_, one_, ALU.add))
                link(TT(d_, d_, ln_, ALU.mult))
                link(TT(d_, d_, e_, ALU.mult))
                TS(lru_k, d_, -LRU_C, None, ALU.mult).then_inc(par_ready, 1)

            def modulation(i):
                v = slice(24 * i, 24 * i + 24)
                dve.wait_ge(mod_cols, i + 1)
                TT(modT[:, v], PB[:, 2, 0:24], C("mod_b", 24 * i, 24), ALU.add).then_inc(mod_copied, 1)
                dve.wait_ge(mod_copied, i + 1)
                v = slice(24 * i + 8, 24 * i + 16)
                link(TS(modT[:, v], modT[:, v], 1.0, None, ALU.add))

            roots = [0]

            def rstd():
                roots[0] += 1
                dve.wait_ge(root_done, roots[0])
                link(dve.reciprocal(rs, rs))

            def pre(b):
                if b < SECOND:
                    rstd()
                    for t in range(NT):
                        last = TS(XN[:, t, :], X[:, t, :], rs[:, t:t + 1], None, ALU.mult)
                    last.then_inc(xn_done, 1)
                m = 48 * ((b - SECOND) // 2) + 24 * (b % 2)
                for j in range(4):
                    dve.wait_ge(xt_ps, 4 * b + j + 1)
                    for k in (2 * j, 2 * j + 1):
                        src = PB[:, j, (k % 2) * S:(k % 2 + 1) * S]
                        if b < SECOND:
                            last = TS(XTF[:, k, :], src, C("norm_pre", 8 * b + k), None, ALU.mult)
                        else:
                            last = TS(XTF[:, k, :], src, modT[:, m + 8 + k:m + 9 + k], modT[:, m + k:m + k + 1],
                                      ALU.mult, ALU.add)
                    last.then_inc(xt_f, 1)
                for j in range(4):
                    dve.wait_ge(xt_h, 4 * b + j + 1)
                    TT(XL[:, 2 * j:2 * j + 2, :], XTF[:, 2 * j:2 * j + 2, :],
                       XH[:, 2 * j:2 * j + 2, :].bitcast(F32), ALU.subtract).then_inc(xt_l, 1)
                dve.wait_ge(xt_l, 4 * (b + 1))

            def post(b):
                if b < SECOND:
                    rstd()
                    dve.wait_ge(gain_in, 16 * (b + 1))
                    for t in range(NT):
                        last = STT(TMP[:, t, :], tile2(PA[:, 2 * t:2 * t + 2, :]), rs[:, t:t + 1], ROW[:, 0:D],
                                   ALU.mult, ALU.mult)
                    link(last)
                    for t in range(NT):
                        last = STT(X[:, t, :], TMP[:, t, :], 1.0 if b in (1, 4) else 0.5, X[:, t, :],
                                   ALU.mult, ALU.add)
                    last.then_inc(x_done, 1)
                    return
                n = b - SECOND
                moe_sum = SUBS[b][0] == "moe"
                dve.wait_ge(gt_ps, n + 1)
                link(TS(ROW[:, 0:D], tile2(PB[:, 2:4, :]), 1.0, None, ALU.add))
                if moe_sum:
                    dve.wait_ge(moe_acc, NE + 1)
                else:
                    dve.wait_ge(d_used, START[b + 1])
                for t in range(NT):
                    y = ACC[:, t, :] if moe_sum else tile2(PA[:, 2 * t:2 * t + 2, :])
                    last = TT(TMP[:, t, :], y, ROW[:, 0:D], ALU.mult)
                link(last)
                for t in range(NT):
                    last = STT(TMP[:, t, :], X[:, t, :], ALPHA, TMP[:, t, :], ALU.mult, ALU.add,
                               accum_out=mu[:, t:t + 1])
                link(last)
                TS(nmu, mu, -1.0 / D, None, ALU.mult).then_inc(mean_done, 1)
                dve.wait_ge(mean_done, n + 1)
                rstd()
                for t in range(NT):
                    last = TS(X[:, t, :], TMP[:, t, :], nmu[:, t:t + 1], rs[:, t:t + 1], ALU.add, ALU.mult)
                link(last)
                dve.wait_ge(ln_in, 32 * (n + 1))
                for t in range(NT):
                    last = TT(X[:, t, :], X[:, t, :], ROW[:, D:2 * D], ALU.mult)
                link(last)
                for t in range(NT):
                    last = TT(X[:, t, :], X[:, t, :], ROW[:, 2 * D:3 * D], ALU.add)
                last.then_inc(x_done, 1)

            def ffn(n0, dyn, nf, f0, fdyn):
                steps, reg = chain.n, chain.reg
                with dve.Fori(0, nf // 2) as j:
                    at, chain.n, chain.reg = dyn + j * 2, steps, reg + j * 4
                    for r, n in enumerate((n0, n0 + 1)):
                        k = n % 2
                        lo_gu(n + 1, at)
                        dve.wait_ge(silu_done, fdyn + j * 2 + (f0 + r + 1))
                        link(TT(HF[k], SG[k], PB[:, k, S:2 * S], ALU.mult))
                        link(dve.tensor_copy(HH[k][:, :], HF[k]))
                        TT(HL[k][:, :], HF[k], HH[k][:, :].bitcast(F32), ALU.subtract).then_inc(h_ready, 1)
                        lo_d(n + 1, at)
                chain.n, chain.reg = steps + 2 * nf, reg

            mixed = [0]

            def mix_lo(dst, src, hi_part):
                mixed[0] += 1
                dve.wait_ge(mix_h, mixed[0])
                TT(dst, src, hi_part.bitcast(F32), ALU.subtract).then_inc(mix_l, 1)

            def product(n, part):
                dve.wait_ge(d_used if part == 2 else gu_used, n + 1)

            def evac(b, i, copy, n, part):
                product(n, part)
                copy(PB[:, (TSTART[b] + i) % 4, 0:S]).then_inc(t_evac, 1)

            def to(dst):
                return lambda ps: dve.tensor_copy(dst, ps)

            def ab(b):
                U = START[b]
                copies = [to(QK[:, k, :]) for k in range(8)] + [to(LX[:, k, 4:260]) for k in range(4)] + \
                         [to(LG[:, k * S:(k + 1) * S]) for k in range(4)]
                link(dve.memset(LX[:, :, 0:4], 0.0))
                i = 0
                for u, blocks in enumerate(((0, 1, 2), (0, 1, 2), (0, 1), (), (0, 1, 2), (0, 1, 2), (0, 2))):
                    lo(U + u + 1)
                    for part in blocks:
                        evac(b, i, copies[i], U + u, part)
                        i += 1
                    if u == 3:
                        product(U + 3, 2)
                        dve.tensor_copy(VA, PA[:, 0:2, :]).then_inc(a["v_sb"], 1)
                dve.wait_ge(t_evac, TSTART[b + 1])
                dve.wait_ge(a["rot"], 1)
                cosb, sinb = (K(n).unsqueeze(1).broadcast_to([P, 8, S]) for n in ("cos", "sin"))
                link(TT(ROT, PB[:, :, :].rearrange("p a (c s) -> p (a c) s", c=2), sinb, ALU.mult))
                link(TT(QK, QK, cosb, ALU.mult))
                TT(QK, QK, ROT, ALU.add).then_inc(a["roped"], 1)
                for t in range(4):
                    xc = XC[:, t * S:(t + 1) * S]
                    link(TS(xc, LX[:, t, 1:257], C("conv_w", t), C("conv_b", t), ALU.mult, ALU.add))
                    link(STT(xc, LX[:, t, 2:258], C("conv_w", 4 + t), xc, ALU.mult, ALU.add))
                    link(STT(xc, LX[:, t, 3:259], C("conv_w", 8 + t), xc, ALU.mult, ALU.add))
                    STT(xc, LX[:, t, 4:260], C("conv_w", 12 + t), xc, ALU.mult, ALU.add).then_inc(a["conv"], 1)
                for h in range(NH):
                    k, m = h % 2, 2 * (h % 2)
                    dve.wait_ge(a["scores"], h + 1)
                    if h >= 2:
                        dve.wait_ge(a["pT"], h - 1)
                    STT(PR[k], PB[:, k, 0:3 * P], HD ** -0.5, K("amask"), ALU.mult, ALU.add).then_inc(a["masked"], 1)
                    dve.wait_ge(a["masked"], h + 1)
                    dve.reduce_max(smax[:, m:m + 1], PR[k][:, 0:P], AX.X)
                    link(dve.reduce_max(smax[:, m + 1:m + 2], PR[k][:, P:3 * P], AX.X))
                    TS(nmax[:, m:m + 2], smax[:, m:m + 2], -1.0, None, ALU.mult).then_inc(a["nmax"], 1)
                    dve.wait_ge(a["exp"], 2 * h + 2)
                    link(dve.reciprocal(srec[:, m:m + 2], ssum[:, m:m + 2]))
                    TS(PR[k][:, 0:P], PR[k][:, 0:P], srec[:, m:m + 1], None, ALU.mult)
                    TS(PR[k][:, P:3 * P], PR[k][:, P:3 * P], srec[:, m + 1:m + 2], None, ALU.mult).then_inc(a["probs"], 1)
                    if k:
                        mix_lo(ML[:, h // 2, :], PB[:, 2 + (h // 2) % 2, 0:S], MH[:, h // 2, :])
                dve.wait_ge(a["sig"], 4)
                dve.wait_ge(a["conv"], 4)
                for t in range(4):
                    last = TS(RR[:, t * S:(t + 1) * S], RR[:, t * S:(t + 1) * S], lru_k[:, t:t + 1], None, ALU.mult)
                last.then_inc(a["la"], 1)
                dve.wait_ge(a["sig"], 8)
                link(TT(II, II, XC, ALU.mult))
                dve.wait_ge(a["ea"], 2)
                link(TT(RR, AA, AA, ALU.mult))
                STT(TH, RR, 1.0, TH, ALU.add, ALU.mult).then_inc(a["neg"], 1)
                dve.wait_ge(a["root"], 1)
                link(TT(II, II, UU, ALU.mult))
                for t in range(4):
                    v = slice(t * S, (t + 1) * S)
                    last = dve.tensor_tensor_scan(TH[:, v], AA[:, v], II[:, v], 0.0, ALU.mult, ALU.add)
                link(last)
                dve.wait_ge(a["gelu"], 1)
                TT(UU, TH, LG, ALU.mult).then_inc(a["rec"], 1)
                mix_lo(ML[:, 4:8, :], UU.rearrange("p (k s) -> p k s", k=4), MH[:, 4:8, :])
                for u in range(7, 10):
                    lo(U + u + 1)

            def cmix(b):
                U = START[b]
                dve.memset(CM[0][:, 0:2], 0.0)
                link(dve.memset(CM[1][:, 0:2], 0.0))
                for n in range(8):
                    lo(U + n + 1)
                    k = n % 2
                    gate_b, gate_c = c_bank(n, 0), c_bank(n, 1)
                    dve.wait_ge(c_x, n + 1)
                    link(TT(CM[k][:, 2:258], gate_c, CXT[k], ALU.mult))
                    link(TS(CY[k], CM[k][:, 0:256], C("c_conv", n), None, ALU.mult))
                    link(STT(CY[k], CM[k][:, 1:257], C("c_conv", 8 + n), CY[k], ALU.mult, ALU.add))
                    link(STT(CY[k], CM[k][:, 2:258], C("c_conv", 16 + n), CY[k], ALU.mult, ALU.add))
                    TT(CY[k], CY[k], gate_b, ALU.mult).then_inc(c_y, 1)
                    mix_lo(ML[:, n, :], CY[k], MH[:, n, :])
                for u in range(8, 11):
                    lo(U + u + 1)

            def gla(b):
                U, n = START[b], (b - SECOND) // 2
                scaled = [lambda ps, k=k: TS(QG[:, k * S:(k + 1) * S], ps, HD ** -0.5, None, ALU.mult)
                          for k in range(2)]
                copies = scaled + [to(KG[:, 0:S]), to(KG[:, S:2 * S]), to(AL)] + [to(UT[:, t, :]) for t in range(4)]
                i = 0
                dve.wait_ge(s["table"], n + 1)
                for u, blocks in enumerate(((0, 1, 2), (0, 1), (), (), (1, 2), (0, 2))):
                    lo(U + u + 1)
                    for part in blocks:
                        evac(b, i, copies[i], U + u, part)
                        i += 1
                    if u == 4:
                        product(U + 4, 0)
                        dve.tensor_copy(VG, PA[:, 0:2, :]).then_inc(g["vg_sb"], 1)
                        dve.tensor_copy(GO, PA[:, 2:4, :]).then_inc(g["vg_sb"], 1)
                dve.wait_ge(g["z"], n + 1)
                for t in range(2):
                    last = TS(BT[:, t * S:(t + 1) * S], PB[:, t, 0:S], C("alpha_b", 2 * n + t), None, ALU.add)
                link(last)
                STT(LT, BT, -1.0, BT, ALU.mult, ALU.max).then_inc(g["zabs"], 1)
                dve.wait_ge(g["zexp"], 2 * n + 2)
                link(STT(LT, BT, 0.0, LT, ALU.min, ALU.subtract))
                for t in range(2):
                    v = slice(t * S, (t + 1) * S)
                    last = dve.tensor_tensor_scan(BT[:, v], ones.broadcast_to([P, S]), LT[:, v], 0.0,
                                                  ALU.mult, ALU.add)
                link(last)
                masks = K("lmask").rearrange("p (l i) -> p l i", i=P)

                def masked(level, item, pair):
                    m = ident.unsqueeze(1) if level is None else masks[:, level:level + 1, :]
                    m = m.broadcast_to([P, 4, P])
                    dst = SC[:, 0:2] if item == 0 else MT.rearrange("p (w h i) -> p w h i", w=2, h=4)
                    for t in range(2):
                        last = TT(dst[:, t], PB[:, 2 * pair + t, :].rearrange("p (h i) -> p h i", h=4), m, ALU.mult)
                    return last

                dve.wait_ge(g["scores"], 9 * n + 1)
                masked(None, 0, 0).then_inc(g["masked"], 1)
                for j, w in enumerate((P,) + LEVELS):
                    bt, df = (x.rearrange("p (b two s) -> p b two s", two=2, s=w) for x in (BT, DF))
                    ref = bt[:, :, 0, w - 1:w].broadcast_to([P, S // w, w])
                    if j or n:
                        dve.wait_ge(g["qks"], 2 * (8 * n + j))
                    TT(df[:, :, 1, :], bt[:, :, 1, :], ref, ALU.subtract).then_inc(g["diff"], 1)
                    TT(df[:, :, 0, :], ref, bt[:, :, 0, :], ALU.subtract).then_inc(g["diff"], 1)
                    dve.wait_ge(g["scores"], 9 * n + j + 2)
                    if j == 0:
                        dve.tensor_copy(SC[:, 2].rearrange("p h i -> p (h i)").rearrange("p (w x) -> p w x", w=2),
                                        PB[:, 2:4, 0:2 * P]).then_inc(g["masked"], 1)
                        dve.wait_ge(g["masked"], 9 * n + 2)
                    else:
                        link(masked(j - 1, j, (j + 1) % 2))
                        TT(SC[:, 0:2], SC[:, 0:2], MT.rearrange("p (w h i) -> p w h i", w=2, h=4),
                           ALU.add).then_inc(g["masked"], 1)
                        dve.wait_ge(g["masked"], 9 * n + j + 2)
                dve.wait_ge(g["root"], n + 1)
                link(dve.reciprocal(grs, grs))
                for t in range(NT):
                    for h in range(4):
                        last = TS(OG[:, t, h * P:(h + 1) * P], PB[:, t, h * P:(h + 1) * P],
                                  grs[:, 4 * t + h:4 * t + h + 1], None, ALU.mult)
                link(last)
                dve.wait_ge(headgain_in, 16 * (n + 1))
                for t in range(NT):
                    last = TT(OG[:, t, :], OG[:, t, :], HG, ALU.mult)
                link(last)
                dve.wait_ge(g["gout"], n + 1)
                TT(OG, OG, GO, ALU.mult).then_inc(g["og"], 1)
                for t in range(NT):
                    tok = slice(t * P, (t + 1) * P)
                    mix_lo(ML[:, 4:8, tok], PB[:, 2 + t, :].rearrange("p (k s) -> p k s", k=4), MH[:, 4:8, tok])

            def s5(b):
                U, n = START[b], (b - SECOND) // 2
                dve.wait_ge(s5c_in, 16 * (n + 1))
                cr, ci = (s5p[:, i, 16 * n:16 * n + 16].unsqueeze(2).broadcast_to([P, 16, 32]) for i in (25, 26))
                t3 = [x.rearrange("p (t h) -> p t h", h=32) for x in PP]
                TT(t3[0], CRAW[:, 0], cr, ALU.mult)
                TT(t3[1], CRAW[:, 1], ci, ALU.mult)
                TT(t3[2], CRAW[:, 0], ci, ALU.mult)
                link(TT(t3[3], CRAW[:, 1], cr, ALU.mult))
                TT(CS[:, 0], t3[0], t3[1], ALU.subtract)
                TT(CS[:, 1], t3[1], t3[0], ALU.subtract)
                link(TT(CS[:, 2], t3[2], t3[3], ALU.add))
                link(TS(CS[:, 2], CS[:, 2], -1.0, None, ALU.mult))

                def skip(t):
                    dve.wait_ge(s["y"], 8 * n + 2 * t + 2)
                    STT(YT[:, t, :], UT[:, t, :], C("s5_d", 4 * n + t), PB[:, t, 0:S],
                        ALU.mult, ALU.add).then_inc(s["ysum"], 1)

                PP3 = [x.rearrange("p (t s) -> p t s", t=2) for x in PP]
                for r in range(8):
                    R = 8 * n + r
                    er, ei = E[:, 0, 2 * r:2 * r + 2, :], E[:, 1, 2 * r:2 * r + 2, :]
                    vr, vi = (PA[:, 2 * (r % 2) + c, :].rearrange("p (t s) -> p t s", t=2) for c in range(2))
                    dve.wait_ge(s["bu"], R + 1)
                    if r:
                        dve.wait_ge(s["y"], R)
                    TT(PP3[0], vr, er, ALU.mult)
                    TT(PP3[1], vi, ei, ALU.mult)
                    TT(PP3[2], vi, er, ALU.mult)
                    TT(PP3[3], vr, ei, ALU.mult).then_inc(s["bu_used"], 1)
                    dve.wait_ge(s["bu_used"], R + 1)
                    TT(W[:, 0], PP3[0], PP3[1], ALU.add)
                    link(TT(W[:, 1], PP3[2], PP3[3], ALU.subtract))
                    for c in range(2):
                        for t in range(2):
                            at = 16 * n + 2 * r + t
                            last = dve.tensor_tensor_scan(W[:, c, t, :], s5p[:, 14, at:at + 1].broadcast_to([P, S]),
                                                          W[:, c, t, :], 0.0, ALU.mult, ALU.add)
                    link(last)
                    TT(PP3[0], W[:, 0], er, ALU.mult)
                    TT(PP3[1], W[:, 1], ei, ALU.mult)
                    TT(PP3[2], W[:, 1], er, ALU.mult)
                    TT(PP3[3], W[:, 0], ei, ALU.mult).then_inc(s["prod"], 1)
                    if r and r % 2 == 0:
                        skip(r // 2 - 1)
                skip(3)
                dve.wait_ge(s["yh"], n + 1)
                TT(XL[:, 0:4, :], YT, XH[:, 0:4, :].bitcast(F32), ALU.subtract).then_inc(s["yl"], 1)
                lo(U + 7)
                dve.wait_ge(s["sig"], 4 * (n + 1))
                TT(GL, GL, YT, ALU.mult).then_inc(s["gated"], 1)
                mix_lo(ML[:, 0:4, :], GL, MH[:, 0:4, :])
                for u in range(7, 10):
                    lo(U + u + 1)

            def moe(b):
                L, key, oh1, oh2, comb, tmp, bias, w8 = rt
                m1, m2, d, ed, w1, w2 = rt1

                def over(x):
                    return x.unsqueeze(2).broadcast_to([P, NT, NE])

                dve.wait_ge(router_in, 16 * 3)
                dve.wait_ge(logits, 1)
                link(TT(L, PB[:, 2, 0:16].rearrange("p (t e) -> p t e", t=NT), bias, ALU.add))

                def largest(m, one_hot):
                    link(dve.reduce_max(m, L, AX.X))
                    link(TT(key, L, over(m), ALU.is_equal))
                    link(TT(key, key, w8, ALU.mult))
                    link(dve.reduce_max(w2, key, AX.X))
                    link(TT(one_hot, key, over(w2), ALU.is_equal))

                largest(m1, oh1)
                link(TS(tmp, oh1, -1.0, 1.0, ALU.mult, ALU.add))
                link(TT(L, L, tmp, ALU.mult))
                link(STT(L, oh1, -3.0e38, L, ALU.mult, ALU.add))
                largest(m2, oh2)
                TT(d, m2, m1, ALU.subtract).then_inc(route_d, 1)
                dve.wait_ge(route_e, 1)
                link(TS(w2, ed, 1.0, None, ALU.add))
                link(dve.reciprocal(w1, w2))
                link(TT(w2, ed, w1, ALU.mult))
                link(TT(comb, oh1, over(w1), ALU.mult))
                link(TT(tmp, oh2, over(w2), ALU.mult))
                link(TT(comb, comb, tmp, ALU.add))
                dve.memset(ACC, 0.0).then_inc(moe_acc, 1)
                dve.wait_ge(moe_acc, 1)
                steps = chain.n
                with dve.Fori(0, NE) as e:
                    chain.n, chain.reg = steps, e * (2 * NF2)
                    ffn(START[b], e * NF2, NF2, FSTART[b], e * NF2)
                    dve.wait_ge(d_used, e * NF2 + (START[b] + NF2))
                    for t in range(NT):
                        last = STT(ACC[:, t, :], tile2(PA[:, 2 * t:2 * t + 2, :]), comb[:, t, bass.ds(e, 1)],
                                   ACC[:, t, :], ALU.mult, ALU.add)
                    last.then_inc(moe_acc, 1)
                    dve.wait_ge(moe_acc, e + 2)
                chain.n, chain.reg = steps + 2 * NF2 * NE, 0

            parameters()
            lo(0)
            for b, (kind, nf) in enumerate(SUBS):
                pre(b)
                if kind == "ffn":
                    ffn(START[b], 0, nf, FSTART[b], 0)
                    if b in MOD_AT:
                        modulation(MOD_AT.index(b))
                elif kind == "ab":
                    ab(b)
                elif kind == "c":
                    cmix(b)
                elif kind == "mix2":
                    gla(b)
                    s5(b)
                else:
                    moe(b)
                post(b)

        @block.gpsimd
        def _(pool):
            chain = Chain(pool, pool_step)
            link = chain.link
            TT = pool.tensor_tensor

            def table(n):
                pw = s5p[:, 2:4, 16 * n:16 * n + 16]
                t0, t1 = s5p[:, 4, 16 * n:16 * n + 16], s5p[:, 5, 16 * n:16 * n + 16]
                pool.memset(E[:, 0, :, 0:1], 1.0)
                pool.memset(E[:, 1, :, 0:1], 0.0)
                pool.tensor_copy(pw[:, 0], s5p[:, 11, 16 * n:16 * n + 16])
                link(pool.tensor_copy(pw[:, 1], s5p[:, 10, 16 * n:16 * n + 16]))
                w = 1
                while w < S:
                    pr, pi = (pw[:, c].unsqueeze(2).broadcast_to([P, 16, w]) for c in range(2))
                    et = ET[:, 0:16 * w].rearrange("p (t s) -> p t s", t=16)
                    re0, im0 = E[:, 0, :, 0:w], E[:, 1, :, 0:w]
                    re1, im1 = E[:, 0, :, w:2 * w], E[:, 1, :, w:2 * w]
                    TT(re1, re0, pr, ALU.mult)
                    link(TT(et, im0, pi, ALU.mult))
                    link(TT(re1, re1, et, ALU.subtract))
                    TT(im1, re0, pi, ALU.mult)
                    link(TT(et, im0, pr, ALU.mult))
                    link(TT(im1, im1, et, ALU.add))
                    w *= 2
                    if w < S:
                        TT(t0, pw[:, 0], pw[:, 0], ALU.mult)
                        link(TT(t1, pw[:, 1], pw[:, 1], ALU.mult))
                        link(TT(pw[:, 1], pw[:, 0], pw[:, 1], ALU.mult))
                        TT(pw[:, 0], t0, t1, ALU.subtract)
                        link(TT(pw[:, 1], pw[:, 1], pw[:, 1], ALU.add))
                pool.memset(small[:, 6:7], 0.0).then_inc(s["table"], 1)

            def modulation(i):
                if i == 0:
                    pool.wait_ge(c_act_done, 1)
                pool.wait_ge(xt_l, 4 * (MOD_AT[i] + 1))

                def load(n, dyn=0):
                    if i or n >= 3:
                        ge(pool, mod_term, 24 * i + n - 2, dyn)
                    pool.dma_start(MW[n % 3], A["w_mod"][dyn + (24 * i + n)]).then_inc(mod_in[n % 3], 16)

                for n in range(3):
                    load(n)
                for n in range(24):
                    acc, c = MACC[:, (n // 8) * BLK:(n // 8 + 1) * BLK], c_act[:, n % 8:n % 8 + 1]
                    pool.wait_ge(mod_in[n % 3], 16 * (8 * i + n // 3 + 1))
                    if n % 8 == 0:
                        pool.tensor_scalar(acc, MW[n % 3], c, None, ALU.mult).then_inc(mod_term, 1)
                    else:
                        link(pool.tensor_scalar(MW[n % 3], MW[n % 3], c, None, ALU.mult))
                        TT(acc, acc, MW[n % 3], ALU.add).then_inc(mod_term, 1)
                    pool.wait_ge(mod_term, 24 * i + n + 1)
                    if n + 3 < 24:
                        load(n + 3)
                pool.memset(small[:, 7:8], 0.0).then_inc(mod_sums, 1)

            pool.dma_start(rt[6], A["router_b"]).then_inc(router_in, 16)
            pool.dma_start(rt[7], A["first"]).then_inc(router_in, 16)
            pool.dma_start(RW[:, :, :], A["router_w"]).then_inc(router_in, 16)
            for b, (kind, _) in enumerate(SUBS):
                if b < SECOND:
                    if b:
                        pool.wait_ge(x_done, b)
                    pool.dma_start(ROW[:, 0:D], A["norm_post"][b:b + 1, :].broadcast_to([P, D])).then_inc(gain_in, 16)
                    if b == 0:
                        pool.dma_start(LGW, A["lru_gates"]).then_inc(lruw_in, 16)
                    if b in MOD_AT:
                        modulation(MOD_AT.index(b))
                    if b == 5:
                        pool.wait_ge(par_ready, 1)
                        table(0)
                    continue
                n = (b - SECOND) // 2
                pool.wait_ge(x_done, b)
                if kind == "mix2":
                    pool.dma_start(HG, A["head_gain"][n:n + 1, :].broadcast_to([P, 512])).then_inc(headgain_in, 16)
                    pool.dma_start(wau[:, :], A["w_alpha"][n]).then_inc(alphaw_in, 16)
                    for j in range(8):
                        pool.wait_ge(g["exp"], 8 * n + j + 1)
                        if j:
                            pool.wait_ge(g["scores"], 9 * n + j + 1)
                        TT(QS, DF, QG, ALU.mult).then_inc(g["qks"], 1)
                        TT(KS, DF, KG, ALU.mult).then_inc(g["qks"], 1)
                    pool.wait_ge(g["og"], n + 1)
                    pool.dma_start(CRAW, A["s5_c"][n]).then_inc(s5c_in, 16)
                    for r in range(8):
                        if r >= 2:
                            pool.wait_ge(s["bu"], 8 * n + r - 1)
                        pool.dma_start(SBM[r % 2], A["s5_b"][n, r]).then_inc(s5b_in[r % 2], 16)
                    pool.wait_ge(s["y"], 8 * (n + 1))
                pool.dma_start(ROW[:, D:2 * D], A["ln_g"][b - SECOND:b - SECOND + 1, :].broadcast_to([P, D])).then_inc(ln_in, 16)
                pool.dma_start(ROW[:, 2 * D:3 * D], A["ln_b"][b - SECOND:b - SECOND + 1, :].broadcast_to([P, D])).then_inc(ln_in, 16)
                if b in MOD_AT:
                    modulation(MOD_AT.index(b))
                if b == SECOND + 1:
                    table(1)

        @block.tensor
        def _(pe):
            def mm3(out_, w, m, start, stop):
                pe.matmul(out_, w[0], m[0], start=start, stop=False)
                pe.matmul(out_, w[0], m[1], start=False, stop=False)
                return pe.matmul(out_, w[1], m[0], start=False, stop=stop)

            def gu_block(n, half, out_, mh, ml, ks=KD):
                k_ = n % 2
                for k in range(ks):
                    last = mm3(out_, (wh_gu[k_][:, half, k, :], wl_gu[k_][:, half, k, :]),
                               (mh[:, k, :], ml[:, k, :]), k == 0, k == ks - 1)
                return last

            def d_block(n, out_, mh, ml):
                k_ = n % 2
                wh, wl = (w[k_][:, :].rearrange("p (k n) -> p k n", k=KD) for w in (wh_d, wl_d))
                for k in range(KD):
                    last = mm3(out_, (wh[:, k, :], wl[:, k, :]), (mh[:, k, :], ml[:, k, :]), k == 0, k == KD - 1)
                return last

            def flat(n, part):
                k = n % 2
                if part == 2:
                    return wh_d[k][:, :], wl_d[k][:, :]
                return tuple(w[k][:, part].rearrange("p k n -> p (k n)") for w in (wh_gu, wl_gu))

            def row_block(n, part, lhs, start, stop):
                wh, wl = flat(n, part)
                for t in range(NT):
                    for h in range(2):
                        last = mm3(PA[:, 2 * t + h, :], tuple(x[:, t * P:(t + 1) * P] for x in lhs),
                                   (wh[:, h * 512:(h + 1) * 512], wl[:, h * 512:(h + 1) * 512]), start, stop)
                return last

            def pre(b):
                if b < SECOND:
                    pe.wait_ge(xn_done, b + 1)
                else:
                    pe.wait_ge(x_done, b)
                if b == 0:
                    pe.wait_ge(consts_in, 16)
                src = XN if b < SECOND else X
                for j in range(4):
                    for k in (2 * j, 2 * j + 1):
                        for t in range(NT):
                            at = (k % 2) * S + t * P
                            last = pe.transpose(PB[:, j, at:at + P], src[:, t, k * P:(k + 1) * P], ident)
                    last.then_inc(xt_ps, 1)
                pe.wait_ge(xt_l, 4 * (b + 1))

            def gate_rows(b):
                m = 48 * ((b - SECOND) // 2) + 24 * (b % 2) + 16
                if b in MOD_AT:
                    pe.wait_ge(mod_copied, MOD_AT.index(b) + 1)
                for k in range(KD):
                    last = pe.matmul(PB[:, 2 + k // 4, (k % 4) * P:(k % 4 + 1) * P],
                                     modT[:, m + k:m + k + 1].broadcast_to([P, P]), ident, start=True, stop=True)
                last.then_inc(gt_ps, 1)

            def gate_up(n, dyn=0):
                ge(pe, gu_lo, n + 1, dyn)
                gu_block(n, 0, PB[:, n % 2, 0:S], XH, XL)
                gu_block(n, 1, PB[:, n % 2, S:2 * S], XH, XL).then_inc(gu_used, 1)

            def down(n, dyn, f, fdyn, start, stop):
                ge(pe, d_lo, n + 1, dyn)
                ge(pe, h_ready, f + 1, fdyn)
                row_block(n, 2, (HH[n % 2], HL[n % 2]), start, stop).then_inc(d_used, 1)

            def mod_columns(i):
                pe.wait_ge(mod_sums, i + 1)
                for k in range(24):
                    last = pe.matmul(PB[:, 2, k:k + 1], MACC[:, k * P:(k + 1) * P], ones, start=True, stop=True)
                last.then_inc(mod_cols, 1)

            def ffn(n0, dyn, nf, f0, fdyn):
                gate_up(n0, dyn)
                gate_up(n0 + 1, dyn)
                down(n0, dyn, f0, fdyn, True, False)
                with pe.Fori(0, nf // 2 - 1) as j:
                    for r in (2, 3):
                        gate_up(n0 + r, dyn + j * 2)
                        down(n0 + r - 1, dyn + j * 2, f0 + r - 1, fdyn + j * 2, False, False)
                if n0 in MOD_START:
                    mod_columns(MOD_START.index(n0))
                down(n0 + nf - 1, dyn, f0 + nf - 1, fdyn, False, True)

            def unit(n, parts):
                pe.wait_ge(gu_lo, n + 1)
                last = parts[0](n, 0)
                if parts[1]:
                    last = parts[1](n, 1)
                last.then_inc(gu_used, 1)
                pe.wait_ge(d_lo, n + 1)
                parts[2](n, 2).then_inc(d_used, 1)

            count = [0]

            def T(n, part):
                i = count[0]
                count[0] += 1
                if i >= 4:
                    pe.wait_ge(t_evac, i - 3)
                ps = PB[:, i % 4, 0:S]
                return gu_block(n, part, ps, XH, XL) if part < 2 else d_block(n, ps, XH, XL)

            def wide(bank, kk):
                def block_(n, part):
                    wh, wl = (w.rearrange("p (k n) -> p k n", k=2) for w in flat(n, part))
                    for k in range(2):
                        for t in range(NT):
                            m = slice(t * P, (t + 1) * P)
                            last = mm3(PA[:, bank + t, :], (XH[:, 2 * kk + k, m], XL[:, 2 * kk + k, m]),
                                       (wh[:, k, :], wl[:, k, :]), kk == 0 and k == 0, kk == 3 and k == 1)
                    return last
                return block_

            def rows(k, lhs):
                return lambda n, part: row_block(n, part, lhs(k), k == 0, k == KD - 1)

            def mix(k):
                return MH[:, k, :], ML[:, k, :]

            def project(b, first):
                pe.wait_ge(mix_l, MSTART[b + 1])
                r = [rows(k, mix) for k in range(KD)]
                unit(first, r[0:3])
                unit(first + 1, r[3:6])
                unit(first + 2, [r[6], None, r[7]])

            def ab(b):
                U = START[b]
                v = [wide(0, i) for i in range(4)]
                unit(U, [T, T, T])
                unit(U + 1, [T, T, T])
                unit(U + 2, [T, T, v[0]])
                unit(U + 3, v[1:4])
                unit(U + 4, [T, T, T])
                unit(U + 5, [T, T, T])
                unit(U + 6, [T, None, T])
                pe.wait_ge(t_evac, 16)
                for k in range(8):
                    last = pe.matmul(PB[:, k // 2, (k % 2) * S:(k % 2 + 1) * S], K("rot"), QK[:, k, :],
                                     start=True, stop=True)
                last.then_inc(a["rot"], 1)
                pe.wait_ge(a["roped"], 1)
                pe.wait_ge(a["v_sb"], 1)

                def scores(h):
                    if h >= 2:
                        pe.wait_ge(a["masked"], h - 1)
                    q, t = slice(64 * (h % 2), 64 * (h % 2) + 64), h // 2
                    pe.matmul(PB[:, h % 2, 0:P], QK[q, t, 0:P], QK[q, 4 + t, 0:P], start=True, stop=True)
                    pe.matmul(PB[:, h % 2, P:3 * P], QK[q, t, P:S], QK[q, 4 + t, :], start=True,
                              stop=True).then_inc(a["scores"], 1)

                scores(0)
                for h in range(NH):
                    if h + 1 < NH:
                        scores(h + 1)
                    pe.wait_ge(a["probs"], h + 1)
                    if h >= 2:
                        pe.wait_ge(a["pT_sb"], h - 1)
                    for i in range(3):
                        last = pe.transpose(PA[:, 2 + h % 2, i * P:(i + 1) * P], PR[h % 2][:, i * P:(i + 1) * P], ident)
                    last.then_inc(a["pT"], 1)
                    pe.wait_ge(a["pT_sb"], h + 1)
                    if h >= 4 and h % 2 == 0:
                        pe.wait_ge(mix_l, h // 2 - 1)
                    o = PB[64 * (h % 2):64 * (h % 2) + 64, 2 + (h // 2) % 2, :]
                    v0, v1 = (VA[:, t, h * HD:(h + 1) * HD] for t in range(2))
                    pe.matmul(o[:, 0:P], v0, PT[h % 2][:, 0:P], start=True, stop=True)
                    pe.matmul(o[:, P:S], v0, PT[h % 2][:, P:2 * P], start=True, stop=False)
                    pe.matmul(o[:, P:S], v1, PT[h % 2][:, 2 * P:3 * P], start=False, stop=True).then_inc(a["av"], 1)
                pe.wait_ge(lruw_in, 16)
                pe.wait_ge(a["conv"], 4)
                pe.wait_ge(mix_l, 4)
                pe.wait_ge(a["pT_sb"], NH)
                for gate in range(2):
                    for t in range(4):
                        pe.matmul((PB if gate == 0 else PA)[:, t, 0:S], LGW[:, gate, t, :], XC[:, t * S:(t + 1) * S],
                                  start=True, stop=True).then_inc(a["gates"], 1)
                project(b, U + 7)

            def cmix(b):
                U = START[b]
                for n in range(8):
                    if n >= 2:
                        pe.wait_ge(c_y, n - 1)

                    def tile(i, n=n):
                        return lambda u, part: (gu_block(u, part, c_bank(n, i), XH, XL) if part < 2
                                                else d_block(u, c_bank(n, i), XH, XL))
                    unit(U + n, [tile(0), tile(1), tile(2)])
                project(b, U + 8)

            def mix2(b):
                U, n = START[b], (b - SECOND) // 2
                v, go = ([wide(bank, i) for i in range(4)] for bank in (0, 2))
                unit(U, [T, T, T])
                unit(U + 1, [T, T, v[0]])
                unit(U + 2, v[1:4])
                unit(U + 3, go[0:3])
                unit(U + 4, [go[3], T, T])
                unit(U + 5, [T, None, T])
                pe.wait_ge(t_evac, TSTART[b + 1])
                pe.wait_ge(alphaw_in, 16 * (n + 1))
                for t in range(2):
                    last = pe.matmul(PB[:, t, 0:S], wau[:, t * P:(t + 1) * P], AL[0:16, :], start=True, stop=True)
                last.then_inc(g["z"], 1)

                def pair_scores(q, k, pair):
                    for t in range(2):
                        for h in range(4):
                            hp, tok = slice(64 * (h % 2), 64 * (h % 2) + 64), (h // 2) * S + t * P
                            at = (2 * t + h // 2) * P
                            last = pe.matmul(PB[:, 2 * pair + h % 2, at:at + P], k[hp, tok:tok + P],
                                             q[hp, tok:tok + P], start=True, stop=True)
                    return last

                pe.wait_ge(g["zabs"], n + 1)
                pair_scores(QG, KG, 0).then_inc(g["scores"], 1)
                for j in range(8):
                    pe.wait_ge(g["qks"], 2 * (8 * n + j + 1))
                    if j:
                        pe.wait_ge(g["masked"], 9 * n + j)
                        pair_scores(QS, KS, (j + 1) % 2).then_inc(g["scores"], 1)
                        continue
                    for h in range(4):
                        hp, tok = slice(64 * (h % 2), 64 * (h % 2) + 64), (h // 2) * S
                        at = (h // 2) * P
                        last = pe.matmul(PB[:, 2 + h % 2, at:at + P], KS[hp, tok:tok + P], QS[hp, tok + P:tok + S],
                                         start=True, stop=True)
                    last.then_inc(g["scores"], 1)
                pe.wait_ge(g["masked"], 9 * (n + 1))
                pe.wait_ge(g["vg_sb"], 2 * (n + 1))
                for h in range(4):
                    v0, v1 = (VG[:, t, h * P:(h + 1) * P] for t in range(2))
                    o = slice(h * P, (h + 1) * P)
                    odd, r = h % 2, h // 2
                    pe.matmul(PB[:, 0, o], SC[:, odd, r, :], v0, start=True, stop=True)
                    pe.matmul(PB[:, 1, o], SC[:, 2, 2 * odd + r, :], v0, start=True, stop=False)
                    last = pe.matmul(PB[:, 1, o], SC[:, odd, 2 + r, :], v1, start=False, stop=True)
                last.then_inc(g["o"], 1)
                pe.wait_ge(g["og"], n + 1)
                for t in range(NT):
                    for k in range(4):
                        last = pe.transpose(PB[:, 2 + t, k * P:(k + 1) * P], OG[:, t, k * P:(k + 1) * P], ident)
                    last.then_inc(g["oT"], 1)

                def bu(r):
                    R = 8 * n + r
                    pe.wait_ge(s5b_in[r % 2], 16 * (4 * n + r // 2 + 1))
                    if r >= 2:
                        pe.wait_ge(s["bu_used"], R - 1)
                    for c in range(2):
                        for t in range(2):
                            last = pe.matmul(PA[:, 2 * (r % 2) + c, t * S:(t + 1) * S], SBM[r % 2][:, c, t, :],
                                             UT[:, r // 2, :], start=True, stop=True)
                    last.then_inc(s["bu"], 1)

                bu(0)
                pe.wait_ge(mix_l, MSTART[b] + 2)
                for r in range(8):
                    if r + 1 < 8:
                        bu(r + 1)
                    pe.wait_ge(s["prod"], 8 * n + r + 1)
                    for t in range(2):
                        st = 2 * r + t
                        o = PB[32 * (st % 4):32 * (st % 4) + 32, r // 2, 0:S]
                        for i, c in enumerate((0, 1, 2, 2)):
                            last = pe.matmul(o, CS[:, c, st, :], PP[i][:, t * S:(t + 1) * S], start=i == 0, stop=i == 3)
                    last.then_inc(s["y"], 1)

                pe.wait_ge(s["yl"], n + 1)
                pe.wait_ge(s["ysum"], 4 * (n + 1))

                def glu(j):
                    def block_(n_, part):
                        wh, wl = (w.rearrange("p (k n) -> p k n", k=4) for w in flat(n_, part))
                        for c in range(2):
                            m = slice(c * P, (c + 1) * P)
                            for k in range(4):
                                last = mm3(PB[:, 2 * j + c, 0:S], (wh[:, k, m], wl[:, k, m]),
                                           (XH[:, k, :], XL[:, k, :]), k == 0, k == 3)
                        return last
                    return block_

                unit(U + 6, [glu(0), None, glu(1)])
                project(b, U + 7)

            def moe(b):
                for t in range(NT):
                    for k in range(KD):
                        last = pe.matmul(PB[:, 2, 8 * t:8 * t + 8], XTF[:, k, t * P:(t + 1) * P], RW[:, k, :],
                                         start=k == 0, stop=k == KD - 1)
                last.then_inc(logits, 1)
                with pe.Fori(0, NE) as e:
                    pe.wait_ge(moe_acc, e + 1)
                    ffn(START[b], e * NF2, NF2, FSTART[b], e * NF2)

            for b, (kind, nf) in enumerate(SUBS):
                pre(b)
                if b == len(SUBS) - 1:
                    pe.wait_ge(router_in, 48)
                if kind == "ffn":
                    ffn(START[b], 0, nf, FSTART[b], 0)
                elif kind == "ab":
                    ab(b)
                elif kind == "c":
                    cmix(b)
                elif kind == "mix2":
                    mix2(b)
                else:
                    moe(b)
                if b >= SECOND:
                    gate_rows(b)


def kernel(**inputs):
    import concourse.bacc as bacc
    from concourse.bass_utils import run_bass_kernel_spmd

    I = {k: np.asarray(v) for k, v in inputs.items()}
    w_gu = np.zeros((NU, P, 2, BLK), np.float32)
    w_d = np.zeros((NU, P, BLK), np.float32)

    def put(n, part, block):
        if part == 2:
            w_d[n] = block
        else:
            w_gu[n, :, part] = block

    def tcol(w, j):
        c = w[:, j * P:(j + 1) * P]
        if c.shape[1] < P:
            c = np.pad(c, ((0, 0), (0, P - c.shape[1])))
        return c.reshape(KD, P, P).transpose(1, 0, 2).reshape(P, BLK)

    def wide(w, i):
        return w[2 * i * P:(2 * i + 2) * P].reshape(2, P, 512).transpose(1, 0, 2).reshape(P, BLK)

    def rows(w, k):
        return w[k * P:(k + 1) * P]

    def put_ffn(n, wg, wu, wd):
        for f in range(wg.shape[1] // P):
            put(n + f, 0, tcol(wg, f))
            put(n + f, 1, tcol(wu, f))
            put(n + f, 2, rows(wd, f))

    def put_list(n, blocks):
        for i, blk in enumerate(blocks):
            if blk is not None:
                put(n + i // 3, i % 3, blk)

    w_mod = I["mod_w_2"].reshape(2, KD, P, 6, BLK).transpose(0, 3, 1, 2, 4).reshape(96, P, BLK)
    for b, l, name in ((0, 0, "ffn1"), (2, 0, "ffn2"), (3, 1, "ffn1"), (5, 1, "ffn2")):
        put_ffn(START[b], I[name + "_w_gate"][l], I[name + "_w_up"][l], I[name + "_w_down"][l])
    w, o = I["ab_w_in"][0], I["ab_w_out"][0]
    v = w[:, 1024:1536]
    out3 = lambda o: [rows(o, k) for k in range(7)] + [None, rows(o, 7)]
    put_list(START[1], [tcol(w, j) for j in range(8)] + [wide(v, i) for i in range(4)]
             + [tcol(w, j) for j in range(12, 19)] + [None, tcol(w, 19)] + out3(o))
    w = I["c_w_in"][0]
    put_list(START[4], [tcol(w, 8 * i + j) for j in range(8) for i in range(3)] + out3(I["c_w_out"][0]))
    for l, b in ((0, 6), (1, 8)):
        w, glu = I["w_in_2"][l], I["s5_w_glu_2"][l]
        u, q, k, v, go, al = np.split(w, [512, 768, 1024, 1536, 2048], axis=1)
        gb = [glu[:, 256 * j:256 * j + 256].reshape(4, P, 256).transpose(1, 0, 2).reshape(P, BLK) for j in range(2)]
        put_list(START[b], [tcol(q, 0), tcol(q, 1), tcol(k, 0), tcol(k, 1), tcol(al, 0)]
                 + [wide(v, i) for i in range(4)] + [wide(go, i) for i in range(4)]
                 + [tcol(u, 0), tcol(u, 1), tcol(u, 2), None, tcol(u, 3), gb[0], None, gb[1]] + out3(I["w_out_2"][l]))
    put_ffn(START[7], I["ffn_w_gate_2"][0], I["ffn_w_up_2"][0], I["ffn_w_down_2"][0])
    for e in range(NE):
        put_ffn(START[9] + e * NF2, I["moe_w_gate_2"][0, e], I["moe_w_up_2"][0, e], I["moe_w_down_2"][0, e])

    def cols(x):
        return np.asarray(x, np.float32).reshape(-1, P).T

    parts = {
        "c": cols(I["c_2"][0]), "norm_pre": cols(I["norm_pre"]), "conv_w": cols(I["lru_conv_w"][0]),
        "conv_b": cols(I["lru_conv_b"][0]), "ga_b": cols(I["lru_gate_a_b"]), "gx_b": cols(I["lru_gate_x_b"]),
        "lam": cols(I["lru_lambda"][0]), "c_conv": cols(I["c_conv_w"][0]), "mod_b": cols(I["mod_b_2"]),
        "s5_d": cols(I["s5_d_2"]), "glu_b": cols(I["s5_b_glu_2"]), "alpha_b": cols(I["gla_b_alpha_2"]),
        "re": cols(I["s5_lam_re_2"]), "im": cols(I["s5_lam_im_2"]),
        "ldt": cols(np.repeat(I["s5_log_dt_2"].reshape(-1), 64)),
    }
    col = np.concatenate([parts[n] for n in COLS], axis=1)
    assert col.shape == (P, NCOL)

    half = 8
    inv = 500000.0 ** (-np.arange(0, 16, 2, dtype=np.float32) / np.float32(16))
    ang = np.arange(S, dtype=np.float32)[:, None] * inv.astype(np.float32)[None, :]
    cos, sin, rot = np.ones((P, S), np.float32), np.zeros((P, S), np.float32), np.zeros((P, P), np.float32)
    for base in (0, HD):
        for i in range(half):
            cos[base + i] = cos[base + half + i] = np.cos(ang[:, i])
            sin[base + i] = sin[base + half + i] = np.sin(ang[:, i])
            rot[base + half + i, base + i] = -1.0
            rot[base + i, base + half + i] = 1.0
    i, j = np.arange(P)[:, None], np.arange(P)[None, :]
    neg = np.where(j > i, np.float32(-1e30), np.float32(0))
    amask = np.concatenate([neg, np.zeros((P, P), np.float32), neg], axis=1)
    key, query = i, j
    lm = [((key // (2 * w) == query // (2 * w)) & (key % (2 * w) < w) & (query % (2 * w) >= w)) for w in LEVELS]
    tables = {"ident": np.eye(P), "amask": amask, "cos": cos, "sin": sin, "rot": rot,
              "lmask": np.concatenate(lm, axis=1)}
    consts = np.concatenate([tables[n].astype(np.float32) for n in CONST], axis=1)
    assert consts.shape == (P, NCONST)

    gates = np.zeros((P, 2, 4, P), np.float32)
    for gi, name in enumerate(("lru_gate_a_w", "lru_gate_x_w")):
        for h in range(8):
            r = slice(64 * (h % 2), 64 * (h % 2) + 64)
            gates[r, gi, h // 2, r] = I[name][0, h]
    s5_b = np.zeros((2, 8, P, 2, 2, P), np.float32)
    s5_c = np.zeros((2, P, 2, 16, 32), np.float32)
    for l in range(2):
        for c, (nb, ncm) in enumerate((("s5_b_re_2", "s5_c_re_2"), ("s5_b_im_2", "s5_c_im_2"))):
            for gr in range(32):
                st, half_ = gr // 2, gr % 2
                ch = 16 * gr % P
                s5_b[l, st // 2, ch:ch + 16, c, st % 2, 64 * half_:64 * half_ + 64] = I[nb][l, gr].T
                s5_c[l, 64 * half_:64 * half_ + 64, c, st, 16 * half_:16 * half_ + 16] = I[ncm][l, gr].T
    arrays = {
        "w_gu": w_gu.reshape(NU, P, 2 * BLK), "w_d": w_d, "w_mod": w_mod, "cols": np.ascontiguousarray(col), "consts": consts,
        "x": I["x"][0], "norm_post": I["norm_post"].reshape(6, D), "lru_gates": gates,
        "head_gain": I["gla_head_gain_2"], "w_alpha": I["gla_w_alpha_up_2"], "s5_b": s5_b, "s5_c": s5_c,
        "ln_g": np.stack([I["ln_mix_g_2"], I["ln_ffn_g_2"]], 1).reshape(4, D),
        "ln_b": np.stack([I["ln_mix_b_2"], I["ln_ffn_b_2"]], 1).reshape(4, D),
        "router_w": I["moe_w_router_2"][0].reshape(KD, P, NE).transpose(1, 0, 2).copy(),
        "router_b": np.ascontiguousarray(np.broadcast_to(I["moe_b_router_2"][0], (P, 2, NE))),
        "first": np.ascontiguousarray(np.broadcast_to(np.arange(NE, 0, -1, dtype=np.float32), (P, 2, NE))),
    }
    arrays = {n: np.ascontiguousarray(x) for n, x in arrays.items()}
    nc = bacc.Bacc("TRN2", target_bir_lowering=False, num_devices=1)
    aps = {n: nc.dram_tensor("in_" + n, x.shape, mybir.dt.from_np(x.dtype), kind="ExternalInput").ap()
           for n, x in arrays.items()}
    out = nc.dram_tensor("out", (S, D), F32, kind="ExternalOutput").ap()
    program(nc, aps, out)
    r = run_bass_kernel_spmd(nc, [{"in_" + n: x for n, x in arrays.items()}], core_ids=[0])
    return r.results[0]["out"].reshape(1, S, D)
```

```python
from contextlib import ExitStack

import numpy as np

import concourse.bass as bass
from concourse import mybir

F32 = mybir.dt.float32
F32R = mybir.dt.float32r
I32 = mybir.dt.int32
ALU = mybir.AluOpType
ACT = mybir.ActivationFunctionType
AX = mybir.AxisListType

P = 128
S = 256
NT = S // P
D = 1024
KD = D // P
FF1, FF2 = 2816, 3584
NF1, NF2 = FF1 // P, FF2 // P
HD = 64
NH = 8
NE = 8
BLK = 1024
EPS = 1e-6
LN_EPS = 1e-5
ALPHA = 4.0 ** 0.25
LRU_C = 8.0
TWO_PI = (6.28125, 0.0019350051879882812, 3.0199159819567e-07)
LEVELS = (64, 32, 16, 8, 4, 2, 1)

SUBS = [("ffn", NF1), ("ab", 10), ("ffn", NF1), ("ffn", NF1), ("c", 11), ("ffn", NF1),
        ("mix2", 10), ("ffn", NF2), ("mix2", 10), ("moe", NE * NF2)]
START = [0]
for _, n in SUBS:
    START.append(START[-1] + n)
NU = START[-1] + 2
FSTART = [0]
for kind, n in SUBS:
    FSTART.append(FSTART[-1] + (n if kind in ("ffn", "moe") else 0))

COLS = {}
_at = 0
for name, n in [("c", KD), ("norm_pre", 6 * KD), ("conv_w", 16), ("conv_b", 4), ("ga_b", 4),
                ("gx_b", 4), ("lam", 4), ("c_conv", 3 * KD), ("mod_b", 96), ("s5_d", 8),
                ("glu_b", 8), ("alpha_b", 4), ("re", 32), ("im", 32), ("ldt", 32)]:
    COLS[name] = (_at, n)
    _at += n
NCOL = _at

CONST = {}
_at = 0
for name, n in [("ident", P), ("amask", 3 * P), ("cos", S), ("sin", S), ("rot", P),
                ("lmask", len(LEVELS) * P)]:
    CONST[name] = (_at, n)
    _at += n
NCONST = _at


class Chain:

    def __init__(self, eng, sem):
        self.eng, self.sem, self.n, self.reg = eng, sem, 0, 0

    def link(self, ins):
        self.n += 1
        ins.then_inc(self.sem, 1)
        self.eng.wait_ge(self.sem, self.reg + self.n)


def ge(eng, sm, n, dyn=0):
    if not isinstance(dyn, int):
        eng.wait_ge(sm, dyn + n)
    elif n + dyn > 0:
        eng.wait_ge(sm, n + dyn)


def program(nc, A, out):
    with ExitStack() as ctx:
        def sb(name, shape, dt=F32):
            return ctx.enter_context(nc.sbuf_tensor(name, shape, dt))

        def sem(name):
            return ctx.enter_context(nc.semaphore(name))

        raw_gu = [sb(f"raw_gu{i}", [P, 2 * BLK]) for i in range(2)]
        raw_d = [sb(f"raw_d{i}", [P, BLK]) for i in range(2)]
        wh_gu = [sb(f"wh_gu{i}", [P, 2, KD, P], F32R) for i in range(2)]
        wl_gu = [sb(f"wl_gu{i}", [P, 2, KD, P], F32R) for i in range(2)]
        wh_d = [sb(f"wh_d{i}", [P, BLK], F32R) for i in range(2)]
        wl_d = [sb(f"wl_d{i}", [P, BLK], F32R) for i in range(2)]
        X = sb("residual", [P, NT, D])
        XH, XL = sb("xT_hi", [P, KD, S], F32R), sb("xT_lo", [P, KD, S], F32R)
        MH, ML = sb("mixT_hi", [P, KD, S], F32R), sb("mixT_lo", [P, KD, S], F32R)
        ROW = sb("rows", [P, 3 * D])
        cst = sb("const", [P, NCONST])
        col = sb("cols", [P, NCOL])
        HH = [sb(f"h_hi{i}", [P, S], F32R) for i in range(2)]
        HL = [sb(f"h_lo{i}", [P, S], F32R) for i in range(2)]
        modT = sb("modT", [P, 96])
        small = sb("small", [P, 264])
        s5p = sb("s5p", [P, 27, 32])
        s5i = sb("s5i", [P, 32], I32)
        wau = sb("w_alpha", [16, S])
        RW = sb("router_w", [P, KD, NE])
        scr = sb("scratch", [P, 16384])
        PA = ctx.enter_context(nc.psum_tensor("acc", [P, 4, 512], F32))
        PB = ctx.enter_context(nc.psum_tensor("work", [P, 4, 512], F32))

        def C(name, i=0, n=1):
            return col[:, COLS[name][0] + i:COLS[name][0] + i + n]

        def K(name):
            return cst[:, CONST[name][0]:CONST[name][0] + CONST[name][1]]

        ident = K("ident")
        ones, eps_rms, eps_ln = (small[:, i:i + 1] for i in range(3))
        ss, rs, mu, nmu = (small[:, 8 + 2 * i:10 + 2 * i] for i in range(4))
        lru_k, lru_t = small[:, 16:20], [small[:, 20 + 4 * i:24 + 4 * i] for i in range(5)]
        c_act = small[:, 40:48]
        smax, nmax, ssum, srec = (small[:, 48 + 4 * i:52 + 4 * i] for i in range(4))
        gss, grs = small[:, 64:72], small[:, 72:80]
        rt = [small[:, 80 + 16 * i:96 + 16 * i].rearrange("p (t e) -> p t e", t=NT) for i in range(8)]
        rt1 = [small[:, 208 + 2 * i:210 + 2 * i] for i in range(6)]

        def view(at, n):
            return scr[:, at:at + n]

        XN = view(0, 2048).rearrange("p (t d) -> p t d", t=NT)
        XTF = view(2048, 2048).rearrange("p (k s) -> p k s", k=KD)
        TMP = view(2048, 2048).rearrange("p (t d) -> p t d", t=NT)
        SG = [view(4096 + 256 * i, 256) for i in range(2)]
        HF = [view(4608 + 256 * i, 256) for i in range(2)]
        ACC = view(5120, 2048).rearrange("p (t d) -> p t d", t=NT)
        JUNK = view(7168, 1024)
        E = view(8192, 8192).rearrange("p (c t s) -> p c t s", c=2, t=16)
        ET = view(5120, 2048)
        MACC = view(0, 3072)
        MW = [view(12288 + 1024 * i, 1024) for i in range(3)]
        QK = view(0, 2048).rearrange("p (k s) -> p k s", k=8)
        LX = view(2048, 1040).rearrange("p (k s) -> p k s", k=4)
        LG, VA = view(3088, 1024), view(4112, 1024).rearrange("p (t d) -> p t d", t=NT)
        PR = [view(5136 + 384 * i, 384) for i in range(2)]
        PT = [view(5904 + 384 * i, 384) for i in range(2)]
        XC, RR, II, AA, TH, UU = (view(6672 + 1024 * i, 1024) for i in range(6))
        ROT = view(12816, 2048).rearrange("p (k s) -> p k s", k=8)
        LGW = ROW[:, 1024:2048].rearrange("p (g t m) -> p g t m", g=2, t=4)
        CXT = [view(256 * i, 256) for i in range(2)]
        CM = [view(512 + 258 * i, 258) for i in range(2)]
        CY = [view(1100 + 256 * i, 256) for i in range(2)]
        UT = view(0, 1024).rearrange("p (k s) -> p k s", k=4)
        QG, KG = view(1024, 512), view(1536, 512)
        AL = view(2048, 256)
        VG = view(2304, 1024).rearrange("p (t d) -> p t d", t=NT)
        GO = view(3328, 1024).rearrange("p (t d) -> p t d", t=NT)
        BT = view(4352, 512)
        first_net = cst[:, CONST["amask"][0]:CONST["lmask"][0]]
        DF = [view(4864, 512), view(7424, 512)]
        QS, KS = ([view(5376 + 512 * i, 512), first_net[:, 512 * i:512 * i + 512]] for i in range(2))
        MT = view(6400, 1024)
        LT = view(7424, 512)
        GJ = view(7936, 128)
        SC = ROW[:, 0:1536].rearrange("p (w h i) -> p w h i", w=3, h=4)
        OG = ROW[:, 1536:2560].rearrange("p (t d) -> p t d", t=NT)
        HG = ROW[:, 2560:3072]
        SBM = [view(1024 + 512 * i, 512).rearrange("p (c t m) -> p c t m", c=2, t=2) for i in range(2)]
        W = view(2048, 1024).rearrange("p (c t s) -> p c t s", c=2, t=2)
        PP = [view(3072 + 512 * i, 512) for i in range(4)]
        TURNED = [[ROW[:, 1536 + 512 * i:2048 + 512 * i] for i in range(3)] + [view(6144, 512)],
                  [view(7168, 512), view(7680, 512), first_net[:, 0:512], first_net[:, 512:1024]]]
        YT = view(5120, 1024).rearrange("p (k s) -> p k s", k=4)
        CRAW = view(6144, 1024).rearrange("p (c t h) -> p c t h", c=2, t=16)
        CS = ROW[:, 0:1536].rearrange("p (c t h) -> p c t h", c=3, t=16)
        GL = view(2048, 1024).rearrange("p (k s) -> p k s", k=4)

        N0, M0 = START[9], FSTART[9]
        RAW_GU = [raw_gu[N0 % 2], raw_gu[(N0 + 1) % 2], view(8192, 2048), view(10240, 2048)]
        RAW_D = [raw_d[N0 % 2], raw_d[(N0 + 1) % 2], view(12288, 1024), view(13312, 1024)]
        YS = view(0, 1024)
        ONE, WGT = (view(1024 + 256 * i, 256).rearrange("p (t i) -> p t i", t=NT) for i in range(2))
        WGT_T = view(1536, 256)
        EARLIER, SLOT = view(1792, P), view(1920, P)
        XGF = view(2048, 1024)
        XGH, XGL = ([x[:, 4 * i:4 * i + 4, :].rearrange("p a (b s) -> p (a b) s", b=2) for i in range(2)]
                    for x in (MH, ML))
        place, share = (small[:, 220 + 20 * i:240 + 20 * i].rearrange("p (t e) -> p t e", t=NT) for i in range(2))
        members = s5i[0:1, 0:NE]

        cols_in, consts_in, x_in, router_in = (sem(n) for n in ("cols_in", "consts_in", "x_in", "router_in"))
        gain_in, lruw_in, ln_in, headgain_in, alphaw_in = (
            sem(n) for n in ("gain_in", "lruw_in", "ln_in", "headgain_in", "alphaw_in"))
        s5b_in, s5c_in = [sem(f"s5b_in{i}") for i in range(2)], sem("s5c_in")
        gu_landed = [sem(f"gu_landed{i}") for i in range(2)]
        d_landed = [sem(f"d_landed{i}") for i in range(2)]
        gu_hi, d_hi, gu_lo, d_lo = sem("gu_hi"), sem("d_hi"), sem("gu_lo"), sem("d_lo")
        gu_used, d_used = sem("gu_used"), sem("d_used")
        dve_step, pool_step = sem("dve_step"), sem("pool_step")
        small_ready, c_act_done = sem("small_ready"), sem("c_act_done")
        par_exp, par_angle, par_trig, par_ready = (sem("par_" + n) for n in ("exp", "angle", "trig", "ready"))
        mod_in = [sem(f"mod_in{i}") for i in range(3)]
        mod_term, mod_sums, mod_cols, mod_copied = (sem("mod_" + n) for n in ("term", "sums", "cols", "copied"))
        silu_done, h_ready = sem("silu_done"), sem("h_ready")
        sq_done, root_done, x_done, mean_done = (sem(n) for n in ("sq_done", "root_done", "x_done", "mean_done"))
        x_first, gained, act_table = sem("x_first"), sem("gained"), sem("act_table")
        xn_done, xt_ps, xt_f, xt_h, xt_l = (sem(n) for n in ("xn_done", "xt_ps", "xt_f", "xt_h", "xt_l"))
        t_evac = sem("t_evac")
        mix_h, mix_l = sem("mix_h"), sem("mix_l")
        gt_ps = sem("gt_ps")
        a = {n: sem("ab_" + n) for n in (
            "v_sb", "rot", "roped", "scores", "masked", "nmax", "exp", "probs", "pT", "pT_sb", "av",
            "conv", "gates", "sig", "la", "ea", "neg", "root", "rec", "gelu")}
        c_x, c_y = sem("c_x_copied"), sem("c_y")
        g = {n: sem("gla_" + n) for n in (
            "vg_sb", "z", "zabs", "zexp", "diff", "exp", "qks", "scores", "masked", "o", "sq",
            "root", "gout", "og", "oT")}
        s = {n: sem("s5_" + n) for n in (
            "table", "c_ready", "bu", "bu_used", "states", "prod", "prod2", "y", "ysum", "gelu", "yh", "yl", "sig", "gated")}
        logits, route_d, route_e, out_done = (sem(n) for n in ("logits", "route_d", "route_e", "out_done"))
        gu_landed4 = [gu_landed[N0 % 2], gu_landed[(N0 + 1) % 2], sem("gu_landed2"), sem("gu_landed3")]
        d_landed4 = [d_landed[N0 % 2], d_landed[(N0 + 1) % 2], sem("d_landed2"), sem("d_landed3")]
        LANDED = [N0 // 2, (N0 + 1) // 2, 0, 0]
        moe_in = sem("moe_tables_in")
        moe_s = {n: sem("moe_" + n) for n in (
            "chosen", "ranks", "routed", "onehots", "gathered", "wT", "xg_f", "xg_h", "xg_l", "y", "scattered",
            "acc", "wT_sb", "hf", "hT", "hh")}

        T_OF = {"ab": 16, "mix2": 9}
        TSTART = [0]
        for kind, _ in SUBS:
            TSTART.append(TSTART[-1] + T_OF.get(kind, 0))
        MIXES = {"ab": 5, "c": 8, "mix2": 3}
        MSTART = [0]
        for kind, _ in SUBS:
            MSTART.append(MSTART[-1] + MIXES.get(kind, 0))
        MOD_AT = [0, 2, 3, 7]
        MOD_START = [START[b] for b in MOD_AT]
        SECOND = 6

        def tile2(x):
            return x.rearrange("p a b -> p (a b)")

        def c_bank(n, i):
            return (PA if n % 2 else PB)[:, i, 0:S]

        block = ctx.enter_context(nc.Block())

        @block.sync
        def _(sp):
            sp.dma_start(col[:, :], A["cols"]).then_inc(cols_in, 16)
            sp.dma_start(cst[:, :], A["consts"]).then_inc(consts_in, 16)

            def load(n, dyn=0):
                k = n % 2
                ge(sp, gu_lo, n - 1, dyn)
                sp.dma_start(raw_gu[k][:, :], A["w_gu"][dyn + n]).then_inc(gu_landed[k], 16)
                ge(sp, d_lo, n - 1, dyn)
                sp.dma_start(raw_d[k][:, :], A["w_d"][dyn + n]).then_inc(d_landed[k], 16)

            sp.dma_start(X[:, :, :], A["x"].rearrange("(t p) d -> p t d", p=P)).then_inc(x_in, 16)
            load(0)
            load(1)
            with sp.Fori(0, (N0 - 2) // 2) as j:
                load(2, j * 2)
                load(3, j * 2)
            if N0 % 2:
                load(N0 - 1)

            def load_moe(i, dyn=0):
                k, n = i % 4, N0 + i
                if i < 2:
                    sp.wait_ge(gu_lo, n - 1)
                elif i < 4:
                    sp.wait_ge(s["ysum"], 8)
                else:
                    ge(sp, gu_lo, n - 3, dyn)
                sp.dma_start(RAW_GU[k] if k > 1 else RAW_GU[k][:, :], A["w_gu"][dyn + n]).then_inc(gu_landed4[k], 16)
                if i >= NE * NF2:
                    return
                if i < 2:
                    sp.wait_ge(d_lo, n - 1)
                elif i >= 4:
                    ge(sp, d_lo, n - 3, dyn)
                sp.dma_start(RAW_D[k] if k > 1 else RAW_D[k][:, :], A["w_d"][dyn + n]).then_inc(d_landed4[k], 16)

            for i in range(4):
                load_moe(i)
            with sp.Fori(0, NE * NF2 // 4 - 1) as j:
                for i in range(4, 8):
                    load_moe(i, j * 4)
            for i in range(NE * NF2, NE * NF2 + 2):
                load_moe(i)
            sp.wait_ge(x_done, len(SUBS))
            sp.dma_start(out.rearrange("(t p) d -> p t d", p=P), X[:, :, :]).then_inc(out_done, 16)
            sp.wait_ge(out_done, 16)

        @block.scalar
        def _(act):
            def hi_gu(n, dyn=0):
                k = n % 2
                act.wait_ge(gu_landed[k], dyn * 8 + 16 * (n // 2 + 1))
                ge(act, gu_used, n - 1, dyn)
                act.activation(wh_gu[k][:, :, :, :].rearrange("p a k n -> p (a k n)"), raw_gu[k][:, :],
                               ACT.Copy).then_inc(gu_hi, 1)

            def hi_d(n, dyn=0):
                k = n % 2
                act.wait_ge(d_landed[k], dyn * 8 + 16 * (n // 2 + 1))
                ge(act, d_used, n - 1, dyn)
                act.activation(wh_d[k][:, :], raw_d[k][:, :], ACT.Copy).then_inc(d_hi, 1)

            def hi(n, dyn=0):
                hi_gu(n, dyn)
                hi_d(n, dyn)

            sums = [0]

            def squares(t, src, bias=None):
                ge(act, sq_done, sums[0])
                act.activation(JUNK, src, ACT.Square, accum_out=ss[:, t:t + 1],
                               **({} if bias is None else {"bias": bias})).then_inc(sq_done, 1)
                sums[0] += 1

            def root(eps, v=slice(0, NT)):
                act.wait_ge(sq_done, sums[0])
                act.activation(rs[:, v], ss[:, v], ACT.Sqrt, bias=eps, scale=1.0 / D).then_inc(root_done, 1)

            tables = [0]

            def load_table(f):
                if tables[0] == 0:
                    act.wait_ge(small_ready, 1)
                else:
                    act.wait_ge(act_table, tables[0])
                act.activation(small[:, 5:6], ones, f).then_inc(act_table, 1)
                tables[0] += 1

            def pre(b):
                if b < SECOND:
                    if b == 0:
                        act.wait_ge(x_in, 16)
                        act.wait_ge(small_ready, 1)
                    for t in range(NT):
                        if b:
                            act.wait_ge(x_done if t else x_first, b)
                        squares(t, X[:, t, :])
                        root(eps_rms, slice(t, t + 1))
                    if SUBS[b][0] == "ffn":
                        load_table(ACT.Silu)
                    for j in range(4):
                        act.wait_ge(xt_ps, 4 * b + j + 1)
                        for k in (2 * j, 2 * j + 1):
                            last = act.activation(XH[:, k, :], PB[:, j, (k % 2) * S:(k % 2 + 1) * S], ACT.Copy,
                                                  scale=C("norm_pre", 8 * b + k))
                        last.then_inc(xt_h, 1)
                    return
                for j in range(4):
                    act.wait_ge(xt_f, 4 * (b - SECOND) + j + 1)
                    act.activation(XH[:, 2 * j:2 * j + 2, :], XTF[:, 2 * j:2 * j + 2, :], ACT.Copy).then_inc(xt_h, 1)

            def post(b):
                load_table(ACT.Sqrt)
                if b < SECOND:
                    act.wait_ge(d_used, START[b + 1])
                    squares(0, tile2(PA[:, 0:2, :]))
                    act.wait_ge(gained, b + 1)
                    squares(1, tile2(PA[:, 2:4, :]))
                    root(eps_rms)
                else:
                    for t in range(NT):
                        act.wait_ge(mean_done, 2 * (b - SECOND) + t + 1)
                        squares(t, TMP[:, t, :], nmu[:, t:t + 1])
                    root(eps_ln)

            def ffn(n0, dyn, nf):
                def steps(at):
                    for n in (n0, n0 + 1):
                        hi_gu(n + 1, at)
                        ge(act, gu_used, n + 1, at)
                        act.activation(SG[n % 2], PB[:, n % 2, 0:S], ACT.Silu).then_inc(silu_done, 1)
                        hi_d(n + 1, at)

                if n0 == 0:
                    steps(0)
                with act.Fori(1 if n0 == 0 else 0, nf // 2) as j:
                    steps(dyn + j * 2)

            def mix_hi(dst, src):
                act.activation(dst, src, ACT.Copy).then_inc(mix_h, 1)

            def ab(b):
                U = START[b]
                for u in range(7):
                    hi(U + u + 1)
                for h in range(NH):
                    act.wait_ge(a["nmax"], h + 1)
                    for q, (at, n) in enumerate(((0, P), (P, S))):
                        m = 2 * (h % 2) + q
                        act.activation(PR[h % 2][:, at:at + n], PR[h % 2][:, at:at + n], ACT.Exp,
                                       bias=nmax[:, m:m + 1], accum_out=ssum[:, m:m + 1]).then_inc(a["exp"], 1)
                    act.wait_ge(a["pT"], h + 1)
                    act.activation(PT[h % 2], PA[:, 2 + h % 2, 0:3 * P], ACT.Copy).then_inc(a["pT_sb"], 1)
                    if h % 2:
                        act.wait_ge(a["av"], h + 1)
                        mix_hi(MH[:, h // 2, :], PB[:, 2 + (h // 2) % 2, 0:S])
                for gate, (dst, bias) in enumerate(((RR, "ga_b"), (II, "gx_b"))):
                    for t in range(4):
                        act.wait_ge(a["gates"], 4 * gate + t + 1)
                        ps = (PB if gate == 0 else PA)[:, t, 0:S]
                        act.activation(dst[:, t * S:(t + 1) * S], ps, ACT.Sigmoid, bias=C(bias, t)).then_inc(a["sig"], 1)
                act.wait_ge(a["la"], 1)
                act.activation(AA, RR, ACT.Exp).then_inc(a["ea"], 1)
                act.activation(TH, RR, ACT.Tanh).then_inc(a["ea"], 1)
                act.wait_ge(a["neg"], 1)
                act.activation(UU, TH, ACT.Sqrt, scale=-1.0).then_inc(a["root"], 1)
                act.activation(LG, LG, ACT.Gelu_apprx_tanh).then_inc(a["gelu"], 1)
                act.wait_ge(a["rec"], 1)
                mix_hi(MH[:, 4:8, :], UU.rearrange("p (k s) -> p k s", k=4))
                for u in range(7, 10):
                    hi(U + u + 1)

            def cmix(b):
                U = START[b]
                for n in range(8):
                    hi(U + n + 1)
                    act.wait_ge(d_used, U + n + 1)
                    act.activation(CXT[n % 2], c_bank(n, 2), ACT.Copy).then_inc(c_x, 1)
                    act.wait_ge(c_y, n + 1)
                    mix_hi(MH[:, n, :], CY[n % 2])
                for u in range(8, 11):
                    hi(U + u + 1)

            def mix2(b):
                U, n = START[b], (b - SECOND) // 2
                for u in range(6):
                    hi(U + u + 1)
                act.wait_ge(g["zabs"], n + 1)
                act.activation(LT, LT, ACT.Exp, scale=-1.0).then_inc(g["zexp"], 1)
                act.wait_ge(g["zexp"], 2 * n + 1)
                act.activation(LT, LT, ACT.Ln, bias=ones).then_inc(g["zexp"], 1)
                for j in range(8):
                    act.wait_ge(g["diff"], 2 * (8 * n + j + 1))
                    act.activation(DF[j % 2], DF[j % 2], ACT.Exp, scale=1.0 / 16.0).then_inc(g["exp"], 1)
                act.wait_ge(g["o"], n + 1)
                for t in range(NT):
                    for h in range(4):
                        ge(act, g["sq"], 8 * n + 4 * t + h)
                        act.activation(GJ, PB[:, t, h * P:(h + 1) * P], ACT.Square,
                                       accum_out=gss[:, 4 * t + h:4 * t + h + 1]).then_inc(g["sq"], 1)
                act.wait_ge(g["sq"], 8 * (n + 1))
                act.activation(grs, gss, ACT.Sqrt, bias=eps_rms, scale=1.0 / P).then_inc(g["root"], 1)
                act.activation(GO, GO, ACT.Silu).then_inc(g["gout"], 1)
                for t in range(NT):
                    act.wait_ge(g["oT"], 2 * n + t + 1)
                    mix_hi(MH[:, 4:8, t * P:(t + 1) * P], PB[:, 2 + t, :].rearrange("p (k s) -> p k s", k=4))
                act.wait_ge(s["ysum"], 4 * (n + 1))
                act.activation(YT, YT, ACT.Gelu_apprx_tanh).then_inc(s["gelu"], 1)
                act.wait_ge(s["gelu"], n + 1)
                act.activation(XH[:, 0:4, :], YT, ACT.Copy).then_inc(s["yh"], 1)
                hi(U + 7)
                for t in range(4):
                    act.wait_ge(gu_used if t < 2 else d_used, U + 7)
                    act.activation(GL[:, t, :], PB[:, t, 0:S], ACT.Sigmoid, bias=C("glu_b", 4 * n + t)).then_inc(s["sig"], 1)
                act.wait_ge(s["gated"], n + 1)
                mix_hi(MH[:, 0:4, :], GL)
                for u in range(7, 9):
                    hi(U + u + 1)
                hi_gu(U + 10)
                if b == SECOND:
                    hi_d(U + 10)

            def moe_hi_gu(i, dyn=0):
                k, n = i % 4, N0 + i
                act.wait_ge(gu_landed4[k], dyn * 4 + 16 * (LANDED[k] + i // 4 + 1))
                act.wait_ge(gu_used, dyn + (n - 1))
                act.activation(wh_gu[n % 2][:, :, :, :].rearrange("p a k n -> p (a k n)"),
                               RAW_GU[k] if k > 1 else RAW_GU[k][:, :], ACT.Copy).then_inc(gu_hi, 1)

            def moe_hi_d(i, dyn):
                k, n = i % 4, N0 + i
                act.wait_ge(d_landed4[k], dyn * 4 + 16 * (LANDED[k] + i // 4 + 1))
                act.wait_ge(d_used, dyn + (n - 1))
                act.activation(wh_d[n % 2][:, :], RAW_D[k] if k > 1 else RAW_D[k][:, :], ACT.Copy).then_inc(d_hi, 1)

            def gathered(i, e=0):
                act.wait_ge(moe_s["gathered"], e + (i + 1))
                c = 48 + 24
                for k in range(KD):
                    last = act.activation(XGF[:, k * P:(k + 1) * P], PB[:, 2 + k // 4, (k % 4) * P:(k % 4 + 1) * P],
                                          ACT.Identity, bias=modT[:, c + k:c + k + 1], scale=modT[:, c + 8 + k:c + 9 + k])
                last.then_inc(moe_s["xg_f"], 1)
                act.wait_ge(moe_s["xg_f"], e + (i + 1))
                act.activation(XGH[i % 2], XGF.rearrange("p (k s) -> p k s", k=KD), ACT.Copy).then_inc(moe_s["xg_h"], 1)

            def moe(b):
                act.wait_ge(route_d, 1)
                act.activation(rt1[3], rt1[2], ACT.Exp).then_inc(route_e, 1)
                moe_hi_gu(1)
                gathered(0)

                def steps(e, width):
                    with act.Fori(0, NF2 // 4) as j:
                        at = e * NF2 + j * 4
                        for i in range(4):
                            n = N0 + i
                            act.wait_ge(gu_used, at + (n + 1))
                            act.activation(SG[n % 2][:, 0:width], PB[:, n % 2, 0:width], ACT.Silu).then_inc(silu_done, 1)
                            moe_hi_gu(i + 2, at)
                            moe_hi_d(i, at)

                with act.Fori(0, NE // 2) as pair:
                    for r in range(2):
                        e = pair * 2 + r
                        gathered(r + 1, pair * 2)
                        count = act.value_load(members[:, bass.ds(e, 1)], min_val=0, max_val=S)
                        with act.If(count <= P):
                            steps(e, P)
                            act.wait_ge(d_used, e * NF2 + (N0 + NF2))
                            act.activation(YS, tile2(PA[:, 0:2, :]), ACT.Copy).then_inc(moe_s["y"], 1)
                        with act.Else():
                            steps(e, S)

            act.wait_ge(cols_in, 16)
            act.activation(c_act, C("c", 0, KD), ACT.Silu).then_inc(c_act_done, 1)
            act.activation(s5p[:, 0, :], C("ldt", 0, 32), ACT.Exp).then_inc(par_exp, 1)
            act.activation(lru_t[0], C("lam", 0, 4), ACT.Exp, scale=-1.0).then_inc(par_exp, 1)
            act.wait_ge(par_angle, 1)
            act.activation(s5p[:, 8, :], s5p[:, 1, :], ACT.Exp).then_inc(par_trig, 1)
            act.activation(s5p[:, 9, :], s5p[:, 1, :], ACT.Tanh, scale=0.5).then_inc(par_trig, 1)
            act.activation(s5p[:, 10, :], s5p[:, 5, :], ACT.Sin).then_inc(par_trig, 1)
            act.activation(s5p[:, 11, :], s5p[:, 6, :], ACT.Sin).then_inc(par_trig, 1)
            act.activation(s5p[:, 12, :], s5p[:, 5, :], ACT.Sin, scale=0.5).then_inc(par_trig, 1)
            act.activation(lru_t[2], lru_t[1], ACT.Ln).then_inc(par_trig, 1)
            hi(0)
            for b, (kind, nf) in enumerate(SUBS):
                pre(b)
                if kind == "ffn":
                    ffn(START[b], 0, nf)
                elif kind == "ab":
                    ab(b)
                elif kind == "c":
                    cmix(b)
                elif kind == "mix2":
                    mix2(b)
                else:
                    moe(b)
                post(b)

        @block.vector
        def _(dve):
            chain = Chain(dve, dve_step)
            link = chain.link
            TT, TS, STT = dve.tensor_tensor, dve.tensor_scalar, dve.scalar_tensor_tensor

            def lo_gu(n, dyn=0):
                k = n % 2
                ge(dve, gu_hi, n + 1, dyn)
                wh, wl = (w[k][:, :, :, :].rearrange("p a k n -> p (a k n)") for w in (wh_gu, wl_gu))
                TT(wl, raw_gu[k][:, :], wh.bitcast(F32), ALU.subtract).then_inc(gu_lo, 1)

            def lo_d(n, dyn=0):
                k = n % 2
                ge(dve, d_hi, n + 1, dyn)
                TT(wl_d[k][:, :], raw_d[k][:, :], wh_d[k][:, :].bitcast(F32), ALU.subtract).then_inc(d_lo, 1)

            def lo(n, dyn=0):
                lo_gu(n, dyn)
                lo_d(n, dyn)

            def parameters():
                dve.memset(ones, 1.0)
                dve.memset(eps_rms, EPS)
                dve.memset(eps_ln, LN_EPS).then_inc(small_ready, 1)
                dve.wait_ge(cols_in, 16)

                def q(i):
                    return s5p[:, i, :]
                re, im = C("re", 0, 32), C("im", 0, 32)
                dve.wait_ge(par_exp, 2)
                TT(q(1), re, q(0), ALU.mult)
                link(TT(q(2), im, q(0), ALU.mult))
                link(TS(s5i[:, :], q(2), 1.0 / (2 * np.pi), None, ALU.mult))
                link(dve.tensor_copy(q(3), s5i[:, :]))
                link(STT(q(4), q(3), -TWO_PI[0], q(2), ALU.mult, ALU.add))
                link(STT(q(4), q(3), -TWO_PI[1], q(4), ALU.mult, ALU.add))
                link(STT(q(4), q(3), -TWO_PI[2], q(4), ALU.mult, ALU.add))
                link(TS(q(5), q(4), 3.1415925, -3.1415925, ALU.min, ALU.max))
                link(STT(q(7), q(5), -1.0, q(5), ALU.mult, ALU.max))
                link(TS(lru_t[1], lru_t[0], 1.0, None, ALU.add))
                TS(q(6), q(7), -1.0, float(np.pi / 2), ALU.mult, ALU.add).then_inc(par_angle, 1)
                dve.wait_ge(par_trig, 6)
                link(STT(q(13), q(8), 1.0, q(9), ALU.add, ALU.mult))
                link(TS(q(14), q(13), 1.0, None, ALU.add))
                TT(q(15), q(13), q(11), ALU.mult)
                link(TT(q(16), q(12), q(12), ALU.mult))
                link(STT(q(17), q(16), -2.0, q(15), ALU.mult, ALU.add))
                link(TT(q(18), q(14), q(10), ALU.mult))
                TT(q(19), re, re, ALU.mult)
                link(TT(q(20), im, im, ALU.mult))
                link(TT(q(19), q(19), q(20), ALU.add))
                link(dve.reciprocal(q(20), q(19)))
                TT(q(21), q(17), re, ALU.mult)
                TT(q(22), q(18), im, ALU.mult)
                TT(q(23), q(18), re, ALU.mult)
                link(TT(q(24), q(17), im, ALU.mult))
                link(TT(q(21), q(21), q(22), ALU.add))
                link(TT(q(23), q(23), q(24), ALU.subtract))
                link(TT(q(25), q(21), q(20), ALU.mult))
                link(TT(q(26), q(23), q(20), ALU.mult))
                e_, w_, ln_, one_, d_ = lru_t
                link(TS(d_, w_, -1.0, None, ALU.add))
                link(TS(one_, d_, 0.0, None, ALU.is_equal))
                link(TT(d_, d_, one_, ALU.add))
                link(dve.reciprocal(d_, d_))
                link(TT(ln_, ln_, one_, ALU.add))
                link(TT(d_, d_, ln_, ALU.mult))
                link(TT(d_, d_, e_, ALU.mult))
                TS(lru_k, d_, -LRU_C, None, ALU.mult).then_inc(par_ready, 1)

            def modulation(i):
                v = slice(24 * i, 24 * i + 24)
                dve.wait_ge(mod_cols, i + 1)
                TT(modT[:, v], PB[:, 2, 0:24], C("mod_b", 24 * i, 24), ALU.add).then_inc(mod_copied, 1)
                dve.wait_ge(mod_copied, i + 1)
                v = slice(24 * i + 8, 24 * i + 16)
                link(TS(modT[:, v], modT[:, v], 1.0, None, ALU.add))

            roots = [0]

            def rstd(v=slice(0, NT)):
                roots[0] += 1
                dve.wait_ge(root_done, roots[0])
                link(dve.reciprocal(rs[:, v], rs[:, v]))

            def pre(b):
                if b < SECOND:
                    for t in range(NT):
                        rstd(slice(t, t + 1))
                        TS(XN[:, t, :], X[:, t, :], rs[:, t:t + 1], None, ALU.mult).then_inc(xn_done, 1)
                    for j in range(4):
                        dve.wait_ge(xt_h, 4 * b + j + 1)
                        for k in (2 * j, 2 * j + 1):
                            last = STT(XL[:, k, :], PB[:, j, (k % 2) * S:(k % 2 + 1) * S], C("norm_pre", 8 * b + k),
                                       XH[:, k, :].bitcast(F32), ALU.mult, ALU.subtract)
                        last.then_inc(xt_l, 1)
                    return
                m = 48 * ((b - SECOND) // 2) + 24 * (b % 2)
                for j in range(4):
                    dve.wait_ge(xt_ps, 4 * b + j + 1)
                    for k in (2 * j, 2 * j + 1):
                        last = TS(XTF[:, k, :], PB[:, j, (k % 2) * S:(k % 2 + 1) * S],
                                  modT[:, m + 8 + k:m + 9 + k], modT[:, m + k:m + k + 1], ALU.mult, ALU.add)
                    last.then_inc(xt_f, 1)
                for j in range(4):
                    dve.wait_ge(xt_h, 4 * b + j + 1)
                    TT(XL[:, 2 * j:2 * j + 2, :], XTF[:, 2 * j:2 * j + 2, :],
                       XH[:, 2 * j:2 * j + 2, :].bitcast(F32), ALU.subtract).then_inc(xt_l, 1)
                dve.wait_ge(xt_l, 4 * (b + 1))

            def post(b):
                if b < SECOND:
                    dve.wait_ge(gain_in, 16 * (b + 1))
                    dve.wait_ge(d_used, START[b + 1])
                    TT(TMP[:, 1, :], tile2(PA[:, 2:4, :]), ROW[:, 0:D], ALU.mult).then_inc(gained, 1)
                    dve.wait_ge(sq_done, 4 * b + 3)
                    link(TT(TMP[:, 0, :], tile2(PA[:, 0:2, :]), ROW[:, 0:D], ALU.mult))
                    rstd()
                    if b not in (1, 4):
                        link(TS(rs, rs, 0.5, None, ALU.mult))
                    for t in range(NT):
                        STT(X[:, t, :], TMP[:, t, :], rs[:, t:t + 1], X[:, t, :],
                            ALU.mult, ALU.add).then_inc(x_done if t else x_first, 1)
                    dve.wait_ge(x_done, b + 1)
                    return
                n = b - SECOND
                moe_sum = SUBS[b][0] == "moe"
                dve.wait_ge(gt_ps, n + 1)
                link(TS(ROW[:, 0:D], tile2(PB[:, 2:4, :]), 1.0, None, ALU.add))
                if moe_sum:
                    dve.wait_ge(moe_s["acc"], NE + 2)
                else:
                    dve.wait_ge(d_used, START[b + 1])
                for t in range(NT):
                    y = ACC[:, t, :] if moe_sum else tile2(PA[:, 2 * t:2 * t + 2, :])
                    last = TT(TMP[:, t, :], y, ROW[:, 0:D], ALU.mult)
                link(last)
                for t in range(NT):
                    link(STT(TMP[:, t, :], X[:, t, :], ALPHA, TMP[:, t, :], ALU.mult, ALU.add,
                             accum_out=mu[:, t:t + 1]))
                    TS(nmu[:, t:t + 1], mu[:, t:t + 1], -1.0 / D, None, ALU.mult).then_inc(mean_done, 1)
                dve.wait_ge(mean_done, 2 * n + 2)
                dve.wait_ge(ln_in, 32 * (n + 1))
                for t in range(NT):
                    last = STT(X[:, t, :], TMP[:, t, :], nmu[:, t:t + 1], ROW[:, D:2 * D], ALU.add, ALU.mult)
                link(last)
                rstd()
                for t in range(NT):
                    STT(X[:, t, :], X[:, t, :], rs[:, t:t + 1], ROW[:, 2 * D:3 * D],
                        ALU.mult, ALU.add).then_inc(x_done if t else x_first, 1)
                dve.wait_ge(x_done, b + 1)

            def ffn(n0, dyn, nf, f0, fdyn):
                steps, reg = chain.n, chain.reg
                with dve.Fori(0, nf // 2) as j:
                    at, chain.n, chain.reg = dyn + j * 2, steps, reg + j * 4
                    for r, n in enumerate((n0, n0 + 1)):
                        k = n % 2
                        lo_gu(n + 1, at)
                        dve.wait_ge(silu_done, fdyn + j * 2 + (f0 + r + 1))
                        link(TT(HF[k], SG[k], PB[:, k, S:2 * S], ALU.mult))
                        link(dve.tensor_copy(HH[k][:, :], HF[k]))
                        TT(HL[k][:, :], HF[k], HH[k][:, :].bitcast(F32), ALU.subtract).then_inc(h_ready, 1)
                        lo_d(n + 1, at)
                chain.n, chain.reg = steps + 2 * nf, reg

            mixed = [0]

            def mix_lo(dst, src, hi_part):
                mixed[0] += 1
                dve.wait_ge(mix_h, mixed[0])
                TT(dst, src, hi_part.bitcast(F32), ALU.subtract).then_inc(mix_l, 1)

            def product(n, part):
                dve.wait_ge(d_used if part == 2 else gu_used, n + 1)

            def evac(b, i, copy, n, part):
                product(n, part)
                copy(PB[:, (TSTART[b] + i) % 4, 0:S]).then_inc(t_evac, 1)

            def to(dst):
                return lambda ps: dve.tensor_copy(dst, ps)

            def ab(b):
                U = START[b]
                copies = [to(QK[:, k, :]) for k in range(8)] + [to(LX[:, k, 4:260]) for k in range(4)] + \
                         [to(LG[:, k * S:(k + 1) * S]) for k in range(4)]
                link(dve.memset(LX[:, :, 0:4], 0.0))
                i = 0
                for u, blocks in enumerate(((0, 1, 2), (0, 1, 2), (0, 1), (), (0, 1, 2), (0, 1, 2), (0, 2))):
                    lo(U + u + 1)
                    for part in blocks:
                        evac(b, i, copies[i], U + u, part)
                        i += 1
                    if u == 3:
                        product(U + 3, 2)
                        dve.tensor_copy(VA, PA[:, 0:2, :]).then_inc(a["v_sb"], 1)
                dve.wait_ge(t_evac, TSTART[b + 1])
                dve.wait_ge(a["rot"], 1)
                cosb, sinb = (K(n).unsqueeze(1).broadcast_to([P, 8, S]) for n in ("cos", "sin"))
                link(TT(ROT, PB[:, :, :].rearrange("p a (c s) -> p (a c) s", c=2), sinb, ALU.mult))
                link(TT(QK, QK, cosb, ALU.mult))
                TT(QK, QK, ROT, ALU.add).then_inc(a["roped"], 1)
                for t in range(4):
                    xc = XC[:, t * S:(t + 1) * S]
                    link(TS(xc, LX[:, t, 1:257], C("conv_w", t), C("conv_b", t), ALU.mult, ALU.add))
                    link(STT(xc, LX[:, t, 2:258], C("conv_w", 4 + t), xc, ALU.mult, ALU.add))
                    link(STT(xc, LX[:, t, 3:259], C("conv_w", 8 + t), xc, ALU.mult, ALU.add))
                    STT(xc, LX[:, t, 4:260], C("conv_w", 12 + t), xc, ALU.mult, ALU.add).then_inc(a["conv"], 1)
                for h in range(NH):
                    k, m = h % 2, 2 * (h % 2)
                    dve.wait_ge(a["scores"], h + 1)
                    if h >= 2:
                        dve.wait_ge(a["pT"], h - 1)
                    STT(PR[k], PB[:, k, 0:3 * P], HD ** -0.5, K("amask"), ALU.mult, ALU.add).then_inc(a["masked"], 1)
                    dve.wait_ge(a["masked"], h + 1)
                    dve.reduce_max(smax[:, m:m + 1], PR[k][:, 0:P], AX.X)
                    link(dve.reduce_max(smax[:, m + 1:m + 2], PR[k][:, P:3 * P], AX.X))
                    TS(nmax[:, m:m + 2], smax[:, m:m + 2], -1.0, None, ALU.mult).then_inc(a["nmax"], 1)
                    dve.wait_ge(a["exp"], 2 * h + 2)
                    link(dve.reciprocal(srec[:, m:m + 2], ssum[:, m:m + 2]))
                    TS(PR[k][:, 0:P], PR[k][:, 0:P], srec[:, m:m + 1], None, ALU.mult)
                    TS(PR[k][:, P:3 * P], PR[k][:, P:3 * P], srec[:, m + 1:m + 2], None, ALU.mult).then_inc(a["probs"], 1)
                    if k:
                        mix_lo(ML[:, h // 2, :], PB[:, 2 + (h // 2) % 2, 0:S], MH[:, h // 2, :])
                dve.wait_ge(a["sig"], 4)
                dve.wait_ge(a["conv"], 4)
                for t in range(4):
                    last = TS(RR[:, t * S:(t + 1) * S], RR[:, t * S:(t + 1) * S], lru_k[:, t:t + 1], None, ALU.mult)
                last.then_inc(a["la"], 1)
                dve.wait_ge(a["sig"], 8)
                link(TT(II, II, XC, ALU.mult))
                dve.wait_ge(a["ea"], 2)
                link(TT(RR, AA, AA, ALU.mult))
                STT(TH, RR, 1.0, TH, ALU.add, ALU.mult).then_inc(a["neg"], 1)
                dve.wait_ge(a["root"], 1)
                link(TT(II, II, UU, ALU.mult))
                for t in range(4):
                    v = slice(t * S, (t + 1) * S)
                    last = dve.tensor_tensor_scan(TH[:, v], AA[:, v], II[:, v], 0.0, ALU.mult, ALU.add)
                link(last)
                dve.wait_ge(a["gelu"], 1)
                TT(UU, TH, LG, ALU.mult).then_inc(a["rec"], 1)
                mix_lo(ML[:, 4:8, :], UU.rearrange("p (k s) -> p k s", k=4), MH[:, 4:8, :])
                for u in range(7, 10):
                    lo(U + u + 1)

            def cmix(b):
                U = START[b]
                dve.memset(CM[0][:, 0:2], 0.0)
                link(dve.memset(CM[1][:, 0:2], 0.0))
                for n in range(8):
                    lo(U + n + 1)
                    k = n % 2
                    gate_b, gate_c = c_bank(n, 0), c_bank(n, 1)
                    dve.wait_ge(c_x, n + 1)
                    link(TT(CM[k][:, 2:258], gate_c, CXT[k], ALU.mult))
                    link(TS(CY[k], CM[k][:, 0:256], C("c_conv", n), None, ALU.mult))
                    link(STT(CY[k], CM[k][:, 1:257], C("c_conv", 8 + n), CY[k], ALU.mult, ALU.add))
                    link(STT(CY[k], CM[k][:, 2:258], C("c_conv", 16 + n), CY[k], ALU.mult, ALU.add))
                    TT(CY[k], CY[k], gate_b, ALU.mult).then_inc(c_y, 1)
                    mix_lo(ML[:, n, :], CY[k], MH[:, n, :])
                for u in range(8, 11):
                    lo(U + u + 1)

            def gla(b):
                U, n = START[b], (b - SECOND) // 2
                scaled = [lambda ps, k=k: TS(QG[:, k * S:(k + 1) * S], ps, HD ** -0.5, None, ALU.mult)
                          for k in range(2)]
                copies = scaled + [to(KG[:, 0:S]), to(KG[:, S:2 * S]), to(AL)] + [to(UT[:, t, :]) for t in range(4)]
                i = 0
                dve.wait_ge(s["table"], n + 1)
                for u, blocks in enumerate(((0, 1, 2), (0, 1), (), (), (1, 2), (0, 2))):
                    lo(U + u + 1)
                    for part in blocks:
                        evac(b, i, copies[i], U + u, part)
                        i += 1
                    if u == 4:
                        product(U + 4, 0)
                        dve.tensor_copy(VG, PA[:, 0:2, :]).then_inc(g["vg_sb"], 1)
                        dve.tensor_copy(GO, PA[:, 2:4, :]).then_inc(g["vg_sb"], 1)
                dve.wait_ge(g["z"], n + 1)
                for t in range(2):
                    last = TS(BT[:, t * S:(t + 1) * S], PB[:, t, 0:S], C("alpha_b", 2 * n + t), None, ALU.add)
                link(last)
                STT(LT, BT, -1.0, BT, ALU.mult, ALU.max).then_inc(g["zabs"], 1)
                dve.wait_ge(g["zexp"], 2 * n + 2)
                link(STT(LT, BT, 0.0, LT, ALU.min, ALU.subtract))
                for t in range(2):
                    v = slice(t * S, (t + 1) * S)
                    last = dve.tensor_tensor_scan(BT[:, v], ones.broadcast_to([P, S]), LT[:, v], 0.0,
                                                  ALU.mult, ALU.add)
                link(last)
                masks = K("lmask").rearrange("p (l i) -> p l i", i=P)

                def masked(level, item, pair):
                    m = ident.unsqueeze(1) if level is None else masks[:, level:level + 1, :]
                    m = m.broadcast_to([P, 4, P])
                    dst = SC[:, 0:2] if item == 0 else MT.rearrange("p (w h i) -> p w h i", w=2, h=4)
                    for t in range(2):
                        last = TT(dst[:, t], PB[:, 2 * pair + t, :].rearrange("p (h i) -> p h i", h=4), m, ALU.mult)
                    return last

                dve.wait_ge(g["scores"], 9 * n + 1)
                masked(None, 0, 0).then_inc(g["masked"], 1)

                def differences(j):
                    w = ((P,) + LEVELS)[j]
                    bt, df = (x.rearrange("p (b two s) -> p b two s", two=2, s=w) for x in (BT, DF[j % 2]))
                    ref = bt[:, :, 0, w - 1:w].broadcast_to([P, S // w, w])
                    if j >= 2:
                        dve.wait_ge(g["qks"], 2 * (8 * n + j - 1))
                    TT(df[:, :, 1, :], bt[:, :, 1, :], ref, ALU.subtract).then_inc(g["diff"], 1)
                    TT(df[:, :, 0, :], ref, bt[:, :, 0, :], ALU.subtract).then_inc(g["diff"], 1)

                for j in range(8):
                    if j == 0:
                        differences(0)
                    if j < 7:
                        differences(j + 1)
                    dve.wait_ge(g["scores"], 9 * n + j + 2)
                    if j == 0:
                        dve.tensor_copy(SC[:, 2].rearrange("p h i -> p (h i)").rearrange("p (w x) -> p w x", w=2),
                                        PB[:, 2:4, 0:2 * P]).then_inc(g["masked"], 1)
                        dve.wait_ge(g["masked"], 9 * n + 2)
                    else:
                        link(masked(j - 1, j, (j + 1) % 2))
                        TT(SC[:, 0:2], SC[:, 0:2], MT.rearrange("p (w h i) -> p w h i", w=2, h=4),
                           ALU.add).then_inc(g["masked"], 1)
                        dve.wait_ge(g["masked"], 9 * n + j + 2)
                dve.wait_ge(g["root"], n + 1)
                link(dve.reciprocal(grs, grs))
                for t in range(NT):
                    for h in range(4):
                        last = TS(OG[:, t, h * P:(h + 1) * P], PB[:, t, h * P:(h + 1) * P],
                                  grs[:, 4 * t + h:4 * t + h + 1], None, ALU.mult)
                link(last)
                dve.wait_ge(headgain_in, 16 * (n + 1))
                for t in range(NT):
                    last = TT(OG[:, t, :], OG[:, t, :], HG, ALU.mult)
                link(last)
                dve.wait_ge(g["gout"], n + 1)
                TT(OG, OG, GO, ALU.mult).then_inc(g["og"], 1)
                for t in range(NT):
                    tok = slice(t * P, (t + 1) * P)
                    mix_lo(ML[:, 4:8, tok], PB[:, 2 + t, :].rearrange("p (k s) -> p k s", k=4), MH[:, 4:8, tok])

            def s5(b):
                U, n = START[b], (b - SECOND) // 2
                dve.wait_ge(s5c_in, 16 * (n + 1))
                cr, ci = (s5p[:, i, 16 * n:16 * n + 16].unsqueeze(2).broadcast_to([P, 16, 32]) for i in (25, 26))
                t3 = [x.rearrange("p (t h) -> p t h", h=32) for x in PP]
                TT(t3[0], CRAW[:, 0], cr, ALU.mult)
                TT(t3[1], CRAW[:, 1], ci, ALU.mult)
                TT(t3[2], CRAW[:, 0], ci, ALU.mult)
                link(TT(t3[3], CRAW[:, 1], cr, ALU.mult))
                TT(CS[:, 0], t3[0], t3[1], ALU.subtract)
                TT(CS[:, 1], t3[1], t3[0], ALU.subtract)
                link(TT(CS[:, 2], t3[2], t3[3], ALU.add))
                link(TS(CS[:, 2], CS[:, 2], -1.0, None, ALU.mult))

                def skip(t):
                    dve.wait_ge(s["y"], 8 * n + 2 * t + 2)
                    STT(YT[:, t, :], UT[:, t, :], C("s5_d", 4 * n + t), PB[:, t, 0:S],
                        ALU.mult, ALU.add).then_inc(s["ysum"], 1)

                PP3 = [x.rearrange("p (t s) -> p t s", t=2) for x in PP]
                for r in range(8):
                    R = 8 * n + r
                    er, ei = E[:, 0, 2 * r:2 * r + 2, :], E[:, 1, 2 * r:2 * r + 2, :]
                    vr, vi = (PA[:, 2 * (r % 2) + c, :].rearrange("p (t s) -> p t s", t=2) for c in range(2))
                    dve.wait_ge(s["bu"], R + 1)
                    TT(PP3[0], vr, er, ALU.mult)
                    TT(PP3[1], vi, ei, ALU.mult)
                    TT(PP3[2], vi, er, ALU.mult)
                    TT(PP3[3], vr, ei, ALU.mult).then_inc(s["bu_used"], 1)
                    dve.wait_ge(s["bu_used"], R + 1)
                    if r:
                        dve.wait_ge(s["prod2"], R)
                    TT(W[:, 0], PP3[0], PP3[1], ALU.add)
                    link(TT(W[:, 1], PP3[2], PP3[3], ALU.subtract))
                    for c in range(2):
                        for t in range(2):
                            at = 16 * n + 2 * r + t
                            last = dve.tensor_tensor_scan(W[:, c, t, :], s5p[:, 14, at:at + 1].broadcast_to([P, S]),
                                                          W[:, c, t, :], 0.0, ALU.mult, ALU.add)
                    last.then_inc(s["states"], 1)
                    dve.wait_ge(s["states"], R + 1)
                    if r >= 2:
                        dve.wait_ge(s["y"], R - 1)
                    q = [x.rearrange("p (t s) -> p t s", t=2) for x in TURNED[r % 2]]
                    TT(q[0], W[:, 0], er, ALU.mult)
                    TT(q[1], W[:, 1], ei, ALU.mult).then_inc(s["prod"], 1)
                    if r and r % 2 == 0:
                        skip(r // 2 - 1)
                skip(3)
                dve.wait_ge(s["yh"], n + 1)
                TT(XL[:, 0:4, :], YT, XH[:, 0:4, :].bitcast(F32), ALU.subtract).then_inc(s["yl"], 1)
                lo(U + 7)
                dve.wait_ge(s["sig"], 4 * (n + 1))
                TT(GL, GL, YT, ALU.mult).then_inc(s["gated"], 1)
                mix_lo(ML[:, 0:4, :], GL, MH[:, 0:4, :])
                for u in range(7, 9):
                    lo(U + u + 1)
                lo_gu(U + 10)
                if b == SECOND:
                    lo_d(U + 10)

            def moe(b):
                L, key, oh1, oh2, comb, tmp, bias, w8 = rt
                m1, m2, d, ed, w1, w2 = rt1

                def over(x):
                    return x.unsqueeze(2).broadcast_to([P, NT, NE])

                dve.wait_ge(router_in, 16 * 3)
                dve.wait_ge(logits, 1)
                link(TT(L, PB[:, 2, 0:16].rearrange("p (t e) -> p t e", t=NT), bias, ALU.add))

                def largest(m, one_hot):
                    link(dve.reduce_max(m, L, AX.X))
                    link(TT(key, L, over(m), ALU.is_equal))
                    link(TT(key, key, w8, ALU.mult))
                    link(dve.reduce_max(w2, key, AX.X))
                    link(TT(one_hot, key, over(w2), ALU.is_equal))

                largest(m1, oh1)
                link(TS(tmp, oh1, -1.0, 1.0, ALU.mult, ALU.add))
                link(TT(L, L, tmp, ALU.mult))
                link(STT(L, oh1, -3.0e38, L, ALU.mult, ALU.add))
                largest(m2, oh2)
                TT(d, m2, m1, ALU.subtract).then_inc(route_d, 1)
                dve.wait_ge(route_e, 1)
                link(TS(w2, ed, 1.0, None, ALU.add))
                link(dve.reciprocal(w1, w2))
                link(TT(w2, ed, w1, ALU.mult))
                link(TT(comb, oh1, over(w1), ALU.mult))
                link(TT(tmp, oh2, over(w2), ALU.mult))
                link(TT(comb, comb, tmp, ALU.add))
                TT(key, oh1, oh2, ALU.add).then_inc(moe_s["chosen"], 1)
                dve.wait_ge(moe_s["chosen"], 1)
                dve.memset(small[:, 220:240], -1.0)
                link(dve.memset(small[:, 240:260], 0.0))
                dve.tensor_copy(share[:, :, 0:NE], comb)
                dve.wait_ge(moe_s["ranks"], 1)
                link(STT(place[:, :, 0:NE], PB[:, 2, 32:48].rearrange("p (t e) -> p t e", t=NT), 1.0, key,
                         ALU.add, ALU.mult))
                TS(place[:, :, 0:NE], place[:, :, 0:NE], -1.0, None, ALU.add)
                dve.memset(ACC, 0.0).then_inc(moe_s["acc"], 1)
                dve.memset(WGT_T, 0.0).then_inc(moe_s["wT_sb"], 1)
                dve.memset(YS, 0.0).then_inc(moe_s["y"], 1)
                dve.tensor_copy(s5i[:, 0:NE], PB[:, 2, 48:56]).then_inc(moe_s["routed"], 1)
                dve.wait_ge(moe_s["routed"], 1)
                dve.wait_ge(moe_in, 32)

                def onehots(dst, e, weight):
                    for t in range(NT):
                        where = place[:, t, bass.ds(e, 1)]
                        if weight:
                            last = TS(dst[:, t], SLOT, where, share[:, t, bass.ds(e, 1)], ALU.is_equal, ALU.mult)
                        else:
                            last = TS(dst[:, t], SLOT, where, None, ALU.is_equal)
                    return last

                def xg_lo(i, e=0):
                    dve.wait_ge(moe_s["xg_h"], e + (i + 1))
                    TT(XGL[i % 2], XGF.rearrange("p (k s) -> p k s", k=KD), XGH[i % 2].bitcast(F32),
                       ALU.subtract).then_inc(moe_s["xg_l"], 1)

                def moe_lo_gu(i, dyn=0):
                    k, n_ = i % 4, N0 + i
                    dve.wait_ge(gu_hi, dyn + (n_ + 1))
                    wh, wl = (w[n_ % 2][:, :, :, :].rearrange("p a k n -> p (a k n)") for w in (wh_gu, wl_gu))
                    TT(wl, RAW_GU[k] if k > 1 else RAW_GU[k][:, :], wh.bitcast(F32), ALU.subtract).then_inc(gu_lo, 1)

                def moe_lo_d(i, dyn):
                    k, n_ = i % 4, N0 + i
                    dve.wait_ge(d_hi, dyn + (n_ + 1))
                    TT(wl_d[n_ % 2][:, :], RAW_D[k] if k > 1 else RAW_D[k][:, :], wh_d[n_ % 2][:, :].bitcast(F32),
                       ALU.subtract).then_inc(d_lo, 1)

                onehots(ONE, 0, False).then_inc(moe_s["onehots"], 1)
                moe_lo_gu(1)
                xg_lo(0)
                onehots(WGT, 0, True)
                onehots(ONE, 1, False).then_inc(moe_s["onehots"], 1)

                def gated(i, at, width):
                    k = (N0 + i) % 2
                    dve.wait_ge(silu_done, at + (M0 + i + 1))
                    TT(HF[k][:, 0:width], SG[k][:, 0:width], PB[:, k, width:2 * width], ALU.mult).then_inc(moe_s["hf"], 1)

                def split(i, at, src, width):
                    k = (N0 + i) % 2
                    dve.tensor_copy(HH[k][:, 0:width], src).then_inc(moe_s["hh"], 1)
                    dve.wait_ge(moe_s["hh"], at + (i + 1))
                    TT(HL[k][:, 0:width], src, HH[k][:, 0:width].bitcast(F32), ALU.subtract).then_inc(h_ready, 1)

                def sparse_step(i, at, first=False, last=False):
                    if not last:
                        gated(i, at, P)
                    if not first:
                        dve.wait_ge(moe_s["hT"], at + i)
                        split(i - 1, at, PB[:, 2 + (N0 + i - 1) % 2, 0:P], P)
                        moe_lo_d(i - 1, at)
                    if not last:
                        moe_lo_gu(i + 2, at)

                def sparse(e):
                    at = e * NF2
                    sparse_step(0, at, first=True)
                    with dve.Fori(0, (NF2 - 4) // 4) as j:
                        for i in range(1, 5):
                            sparse_step(i, at + j * 4)
                    for i in range(NF2 - 3, NF2):
                        sparse_step(i, at)
                    sparse_step(NF2, at, last=True)

                def dense(e, r):
                    with dve.Fori(0, NF2 // 4) as j:
                        at = e * NF2 + j * 4
                        for i in range(4):
                            gated(i, at, S)
                            dve.wait_ge(moe_s["hf"], at + (i + 1))
                            split(i, at, HF[(N0 + i) % 2], S)
                            moe_lo_gu(i + 2, at)
                            moe_lo_d(i, at)
                    dve.wait_ge(d_used, e * NF2 + (N0 + NF2))
                    dve.wait_ge(moe_s["acc"], e + 2)
                    for t in range(NT):
                        STT(ACC[:, t, :], tile2(PA[:, 2 * t:2 * t + 2, :]), share[:, t, bass.ds(e, 1)],
                            ACC[:, t, :], ALU.mult, ALU.add)
                    dve.memset(YS, 0.0).then_inc(moe_s["y"], 1)

                def add_up(count_, scattered_):
                    dve.wait_ge(moe_s["scattered"], scattered_)
                    dve.wait_ge(moe_s["acc"], count_)
                    for t in range(NT):
                        last = TT(ACC[:, t, :], ACC[:, t, :], tile2(PA[:, 2 * t:2 * t + 2, :]), ALU.add)
                    last.then_inc(moe_s["acc"], 1)

                with dve.Fori(0, NE // 2) as pair:
                    for r in range(2):
                        e = pair * 2 + r
                        xg_lo(r + 1, pair * 2)
                        add_up(e + 1, e + 1)
                        dve.wait_ge(moe_s["wT"], e + 1)
                        dve.tensor_copy(WGT_T, PB[:, (N0 + 1) % 2, S:2 * S]).then_inc(moe_s["wT_sb"], 1)
                        onehots(WGT, e + 1, True)
                        onehots(ONE, e + 2, False).then_inc(moe_s["onehots"], 1)
                        count = dve.value_load(members[:, bass.ds(e, 1)], min_val=0, max_val=S)
                        with dve.If(count <= P):
                            sparse(e)
                        with dve.Else():
                            dense(e, r)
                add_up(NE + 1, NE + 1)

            parameters()
            lo(0)
            for b, (kind, nf) in enumerate(SUBS):
                pre(b)
                if kind == "ffn":
                    ffn(START[b], 0, nf, FSTART[b], 0)
                    if b in MOD_AT:
                        modulation(MOD_AT.index(b))
                elif kind == "ab":
                    ab(b)
                elif kind == "c":
                    cmix(b)
                elif kind == "mix2":
                    gla(b)
                    s5(b)
                else:
                    moe(b)
                post(b)

        @block.gpsimd
        def _(pool):
            chain = Chain(pool, pool_step)
            link = chain.link
            TT = pool.tensor_tensor

            def table(n):
                pw = s5p[:, 2:4, 16 * n:16 * n + 16]
                t0, t1 = s5p[:, 4, 16 * n:16 * n + 16], s5p[:, 5, 16 * n:16 * n + 16]
                pool.memset(E[:, 0, :, 0:1], 1.0)
                pool.memset(E[:, 1, :, 0:1], 0.0)
                pool.tensor_copy(pw[:, 0], s5p[:, 11, 16 * n:16 * n + 16])
                link(pool.tensor_copy(pw[:, 1], s5p[:, 10, 16 * n:16 * n + 16]))
                w = 1
                while w < S:
                    pr, pi = (pw[:, c].unsqueeze(2).broadcast_to([P, 16, w]) for c in range(2))
                    et = ET[:, 0:16 * w].rearrange("p (t s) -> p t s", t=16)
                    re0, im0 = E[:, 0, :, 0:w], E[:, 1, :, 0:w]
                    re1, im1 = E[:, 0, :, w:2 * w], E[:, 1, :, w:2 * w]
                    TT(re1, re0, pr, ALU.mult)
                    link(TT(et, im0, pi, ALU.mult))
                    link(TT(re1, re1, et, ALU.subtract))
                    TT(im1, re0, pi, ALU.mult)
                    link(TT(et, im0, pr, ALU.mult))
                    link(TT(im1, im1, et, ALU.add))
                    w *= 2
                    if w < S:
                        TT(t0, pw[:, 0], pw[:, 0], ALU.mult)
                        link(TT(t1, pw[:, 1], pw[:, 1], ALU.mult))
                        link(TT(pw[:, 1], pw[:, 0], pw[:, 1], ALU.mult))
                        TT(pw[:, 0], t0, t1, ALU.subtract)
                        link(TT(pw[:, 1], pw[:, 1], pw[:, 1], ALU.add))
                pool.memset(small[:, 6:7], 0.0).then_inc(s["table"], 1)

            def modulation(i):
                if i == 0:
                    pool.wait_ge(c_act_done, 1)
                pool.wait_ge(xt_l, 4 * (MOD_AT[i] + 1))

                def load(n, dyn=0):
                    if i or n >= 3:
                        ge(pool, mod_term, 24 * i + n - 2, dyn)
                    pool.dma_start(MW[n % 3], A["w_mod"][dyn + (24 * i + n)]).then_inc(mod_in[n % 3], 16)

                for n in range(3):
                    load(n)
                for n in range(24):
                    acc, c = MACC[:, (n // 8) * BLK:(n // 8 + 1) * BLK], c_act[:, n % 8:n % 8 + 1]
                    pool.wait_ge(mod_in[n % 3], 16 * (8 * i + n // 3 + 1))
                    if n % 8 == 0:
                        pool.tensor_scalar(acc, MW[n % 3], c, None, ALU.mult).then_inc(mod_term, 1)
                    else:
                        link(pool.tensor_scalar(MW[n % 3], MW[n % 3], c, None, ALU.mult))
                        TT(acc, acc, MW[n % 3], ALU.add).then_inc(mod_term, 1)
                    pool.wait_ge(mod_term, 24 * i + n + 1)
                    if n + 3 < 24:
                        load(n + 3)
                pool.memset(small[:, 7:8], 0.0).then_inc(mod_sums, 1)

            pool.dma_start(rt[6], A["router_b"]).then_inc(router_in, 16)
            pool.dma_start(rt[7], A["first"]).then_inc(router_in, 16)
            pool.dma_start(RW[:, :, :], A["router_w"]).then_inc(router_in, 16)
            for b, (kind, _) in enumerate(SUBS):
                if b < SECOND:
                    if b:
                        pool.wait_ge(x_done, b)
                    pool.dma_start(ROW[:, 0:D], A["norm_post"][b:b + 1, :].broadcast_to([P, D])).then_inc(gain_in, 16)
                    if b == 0:
                        pool.dma_start(LGW, A["lru_gates"]).then_inc(lruw_in, 16)
                    if b in MOD_AT:
                        modulation(MOD_AT.index(b))
                    if b == 5:
                        pool.wait_ge(par_ready, 1)
                        table(0)
                    continue
                n = (b - SECOND) // 2
                pool.wait_ge(x_done, b)
                if kind == "mix2":
                    pool.dma_start(HG, A["head_gain"][n:n + 1, :].broadcast_to([P, 512])).then_inc(headgain_in, 16)
                    pool.dma_start(wau[:, :], A["w_alpha"][n]).then_inc(alphaw_in, 16)
                    for j in range(8):
                        pool.wait_ge(g["exp"], 8 * n + j + 1)
                        if j >= 2:
                            pool.wait_ge(g["scores"], 9 * n + j)
                        TT(QS[j % 2], DF[j % 2], QG, ALU.mult).then_inc(g["qks"], 1)
                        TT(KS[j % 2], DF[j % 2], KG, ALU.mult).then_inc(g["qks"], 1)
                    pool.wait_ge(g["og"], n + 1)
                    pool.dma_start(CRAW, A["s5_c"][n]).then_inc(s5c_in, 16)
                    for r in range(2):
                        pool.dma_start(SBM[r], A["s5_b"][n, r]).then_inc(s5b_in[r], 16)
                    for r in range(8):
                        R = 8 * n + r
                        pool.wait_ge(s["states"], R + 1)
                        if r >= 2:
                            pool.wait_ge(s["y"], R - 1)
                        q = [x.rearrange("p (t s) -> p t s", t=2) for x in TURNED[r % 2]]
                        TT(q[2], W[:, 1], E[:, 0, 2 * r:2 * r + 2, :], ALU.mult)
                        TT(q[3], W[:, 0], E[:, 1, 2 * r:2 * r + 2, :], ALU.mult).then_inc(s["prod2"], 1)
                        if r + 2 < 8:
                            pool.dma_start(SBM[r % 2], A["s5_b"][n, r + 2]).then_inc(s5b_in[r % 2], 16)
                    pool.wait_ge(s["y"], 8 * (n + 1))
                if kind == "moe":
                    pool.dma_start(EARLIER, A["earlier"]).then_inc(moe_in, 16)
                    pool.dma_start(SLOT, A["slot"]).then_inc(moe_in, 16)
                pool.dma_start(ROW[:, D:2 * D], A["ln_g"][b - SECOND:b - SECOND + 1, :].broadcast_to([P, D])).then_inc(ln_in, 16)
                pool.dma_start(ROW[:, 2 * D:3 * D], A["ln_b"][b - SECOND:b - SECOND + 1, :].broadcast_to([P, D])).then_inc(ln_in, 16)
                if b in MOD_AT:
                    modulation(MOD_AT.index(b))
                if b == SECOND + 1:
                    table(1)

        @block.tensor
        def _(pe):
            def mm3(out_, w, m, start, stop):
                pe.matmul(out_, w[0], m[0], start=start, stop=False)
                pe.matmul(out_, w[0], m[1], start=False, stop=False)
                return pe.matmul(out_, w[1], m[0], start=False, stop=stop)

            def gu_block(n, half, out_, mh, ml, ks=KD):
                k_ = n % 2
                for k in range(ks):
                    last = mm3(out_, (wh_gu[k_][:, half, k, :], wl_gu[k_][:, half, k, :]),
                               (mh[:, k, :], ml[:, k, :]), k == 0, k == ks - 1)
                return last

            def d_block(n, out_, mh, ml):
                k_ = n % 2
                wh, wl = (w[k_][:, :].rearrange("p (k n) -> p k n", k=KD) for w in (wh_d, wl_d))
                for k in range(KD):
                    last = mm3(out_, (wh[:, k, :], wl[:, k, :]), (mh[:, k, :], ml[:, k, :]), k == 0, k == KD - 1)
                return last

            def flat(n, part):
                k = n % 2
                if part == 2:
                    return wh_d[k][:, :], wl_d[k][:, :]
                return tuple(w[k][:, part].rearrange("p k n -> p (k n)") for w in (wh_gu, wl_gu))

            def row_block(n, part, lhs, start, stop):
                wh, wl = flat(n, part)
                for t in range(NT):
                    for h in range(2):
                        last = mm3(PA[:, 2 * t + h, :], tuple(x[:, t * P:(t + 1) * P] for x in lhs),
                                   (wh[:, h * 512:(h + 1) * 512], wl[:, h * 512:(h + 1) * 512]), start, stop)
                return last

            def pre(b):
                if b == 0:
                    pe.wait_ge(consts_in, 16)
                src = XN if b < SECOND else X
                for t in range(NT):
                    if b < SECOND:
                        pe.wait_ge(xn_done, 2 * b + t + 1)
                    else:
                        pe.wait_ge(x_done if t else x_first, b)
                    for k in range(KD):
                        at = (k % 2) * S + t * P
                        last = pe.transpose(PB[:, k // 2, at:at + P], src[:, t, k * P:(k + 1) * P], ident)
                        if t and k % 2:
                            last.then_inc(xt_ps, 1)
                pe.wait_ge(xt_l, 4 * (b + 1))

            def gate_rows(b):
                m = 48 * ((b - SECOND) // 2) + 24 * (b % 2) + 16
                if b in MOD_AT:
                    pe.wait_ge(mod_copied, MOD_AT.index(b) + 1)
                for k in range(KD):
                    last = pe.matmul(PB[:, 2 + k // 4, (k % 4) * P:(k % 4 + 1) * P],
                                     modT[:, m + k:m + k + 1].broadcast_to([P, P]), ident, start=True, stop=True)
                last.then_inc(gt_ps, 1)

            def gate_up(n, dyn=0):
                ge(pe, gu_lo, n + 1, dyn)
                gu_block(n, 0, PB[:, n % 2, 0:S], XH, XL)
                gu_block(n, 1, PB[:, n % 2, S:2 * S], XH, XL).then_inc(gu_used, 1)

            def down(n, dyn, f, fdyn, start, stop):
                ge(pe, d_lo, n + 1, dyn)
                ge(pe, h_ready, f + 1, fdyn)
                row_block(n, 2, (HH[n % 2], HL[n % 2]), start, stop).then_inc(d_used, 1)

            def mod_columns(i):
                pe.wait_ge(mod_sums, i + 1)
                for k in range(24):
                    last = pe.matmul(PB[:, 2, k:k + 1], MACC[:, k * P:(k + 1) * P], ones, start=True, stop=True)
                last.then_inc(mod_cols, 1)

            def ffn(n0, dyn, nf, f0, fdyn):
                gate_up(n0, dyn)
                gate_up(n0 + 1, dyn)
                down(n0, dyn, f0, fdyn, True, False)
                with pe.Fori(0, nf // 2 - 1) as j:
                    for r in (2, 3):
                        gate_up(n0 + r, dyn + j * 2)
                        down(n0 + r - 1, dyn + j * 2, f0 + r - 1, fdyn + j * 2, False, False)
                if n0 in MOD_START:
                    mod_columns(MOD_START.index(n0))
                if n0 == START[SECOND + 1]:
                    gate_rows(SECOND + 1)
                down(n0 + nf - 1, dyn, f0 + nf - 1, fdyn, False, True)

            def unit(n, parts):
                pe.wait_ge(gu_lo, n + 1)
                last = parts[0](n, 0)
                if parts[1]:
                    last = parts[1](n, 1)
                last.then_inc(gu_used, 1)
                pe.wait_ge(d_lo, n + 1)
                parts[2](n, 2).then_inc(d_used, 1)

            count = [0]

            def T(n, part):
                i = count[0]
                count[0] += 1
                if i >= 4:
                    pe.wait_ge(t_evac, i - 3)
                ps = PB[:, i % 4, 0:S]
                return gu_block(n, part, ps, XH, XL) if part < 2 else d_block(n, ps, XH, XL)

            def wide(bank, kk):
                def block_(n, part):
                    wh, wl = (w.rearrange("p (k n) -> p k n", k=2) for w in flat(n, part))
                    for k in range(2):
                        for t in range(NT):
                            m = slice(t * P, (t + 1) * P)
                            last = mm3(PA[:, bank + t, :], (XH[:, 2 * kk + k, m], XL[:, 2 * kk + k, m]),
                                       (wh[:, k, :], wl[:, k, :]), kk == 0 and k == 0, kk == 3 and k == 1)
                    return last
                return block_

            def rows(k, lhs):
                return lambda n, part: row_block(n, part, lhs(k), k == 0, k == KD - 1)

            def mix(k):
                return MH[:, k, :], ML[:, k, :]

            def project(b, first):
                pe.wait_ge(mix_l, MSTART[b + 1])
                r = [rows(k, mix) for k in range(KD)]
                unit(first, r[0:3])
                if b >= SECOND:
                    pe.wait_ge(s["sig"], 4 * (b - SECOND) // 2 + 4)
                    gate_rows(b)
                unit(first + 1, r[3:6])
                unit(first + 2, [r[6], None, r[7]])

            def ab(b):
                U = START[b]
                v = [wide(0, i) for i in range(4)]
                unit(U, [T, T, T])
                unit(U + 1, [T, T, T])
                unit(U + 2, [T, T, v[0]])
                unit(U + 3, v[1:4])
                unit(U + 4, [T, T, T])
                unit(U + 5, [T, T, T])
                unit(U + 6, [T, None, T])
                pe.wait_ge(t_evac, 16)
                for k in range(8):
                    last = pe.matmul(PB[:, k // 2, (k % 2) * S:(k % 2 + 1) * S], K("rot"), QK[:, k, :],
                                     start=True, stop=True)
                last.then_inc(a["rot"], 1)
                pe.wait_ge(a["roped"], 1)
                pe.wait_ge(a["v_sb"], 1)

                def scores(h):
                    if h >= 2:
                        pe.wait_ge(a["masked"], h - 1)
                    q, t = slice(64 * (h % 2), 64 * (h % 2) + 64), h // 2
                    pe.matmul(PB[:, h % 2, 0:P], QK[q, t, 0:P], QK[q, 4 + t, 0:P], start=True, stop=True)
                    pe.matmul(PB[:, h % 2, P:3 * P], QK[q, t, P:S], QK[q, 4 + t, :], start=True,
                              stop=True).then_inc(a["scores"], 1)

                scores(0)
                for h in range(NH):
                    if h + 1 < NH:
                        scores(h + 1)
                    pe.wait_ge(a["probs"], h + 1)
                    if h >= 2:
                        pe.wait_ge(a["pT_sb"], h - 1)
                    for i in range(3):
                        last = pe.transpose(PA[:, 2 + h % 2, i * P:(i + 1) * P], PR[h % 2][:, i * P:(i + 1) * P], ident)
                    last.then_inc(a["pT"], 1)
                    pe.wait_ge(a["pT_sb"], h + 1)
                    if h >= 4 and h % 2 == 0:
                        pe.wait_ge(mix_l, h // 2 - 1)
                    o = PB[64 * (h % 2):64 * (h % 2) + 64, 2 + (h // 2) % 2, :]
                    v0, v1 = (VA[:, t, h * HD:(h + 1) * HD] for t in range(2))
                    pe.matmul(o[:, 0:P], v0, PT[h % 2][:, 0:P], start=True, stop=True)
                    pe.matmul(o[:, P:S], v0, PT[h % 2][:, P:2 * P], start=True, stop=False)
                    pe.matmul(o[:, P:S], v1, PT[h % 2][:, 2 * P:3 * P], start=False, stop=True).then_inc(a["av"], 1)
                pe.wait_ge(lruw_in, 16)
                pe.wait_ge(a["conv"], 4)
                pe.wait_ge(mix_l, 4)
                pe.wait_ge(a["pT_sb"], NH)
                for gate in range(2):
                    for t in range(4):
                        pe.matmul((PB if gate == 0 else PA)[:, t, 0:S], LGW[:, gate, t, :], XC[:, t * S:(t + 1) * S],
                                  start=True, stop=True).then_inc(a["gates"], 1)
                project(b, U + 7)

            def cmix(b):
                U = START[b]
                for n in range(8):
                    if n >= 2:
                        pe.wait_ge(c_y, n - 1)

                    def tile(i, n=n):
                        return lambda u, part: (gu_block(u, part, c_bank(n, i), XH, XL) if part < 2
                                                else d_block(u, c_bank(n, i), XH, XL))
                    unit(U + n, [tile(0), tile(1), tile(2)])
                project(b, U + 8)

            def mix2(b):
                U, n = START[b], (b - SECOND) // 2
                v, go = ([wide(bank, i) for i in range(4)] for bank in (0, 2))
                unit(U, [T, T, T])
                unit(U + 1, [T, T, v[0]])
                unit(U + 2, v[1:4])
                unit(U + 3, go[0:3])
                unit(U + 4, [go[3], T, T])
                unit(U + 5, [T, None, T])
                pe.wait_ge(t_evac, TSTART[b + 1])
                pe.wait_ge(alphaw_in, 16 * (n + 1))
                for t in range(2):
                    last = pe.matmul(PB[:, t, 0:S], wau[:, t * P:(t + 1) * P], AL[0:16, :], start=True, stop=True)
                last.then_inc(g["z"], 1)

                def pair_scores(q, k, pair):
                    for t in range(2):
                        for h in range(4):
                            hp, tok = slice(64 * (h % 2), 64 * (h % 2) + 64), (h // 2) * S + t * P
                            at = (2 * t + h // 2) * P
                            last = pe.matmul(PB[:, 2 * pair + h % 2, at:at + P], k[hp, tok:tok + P],
                                             q[hp, tok:tok + P], start=True, stop=True)
                    return last

                pe.wait_ge(g["zabs"], n + 1)
                pair_scores(QG, KG, 0).then_inc(g["scores"], 1)
                for j in range(8):
                    pe.wait_ge(g["qks"], 2 * (8 * n + j + 1))
                    if j:
                        pe.wait_ge(g["masked"], 9 * n + j)
                        pair_scores(QS[j % 2], KS[j % 2], (j + 1) % 2).then_inc(g["scores"], 1)
                        continue
                    for h in range(4):
                        hp, tok = slice(64 * (h % 2), 64 * (h % 2) + 64), (h // 2) * S
                        at = (h // 2) * P
                        last = pe.matmul(PB[:, 2 + h % 2, at:at + P], KS[0][hp, tok:tok + P], QS[0][hp, tok + P:tok + S],
                                         start=True, stop=True)
                    last.then_inc(g["scores"], 1)
                pe.wait_ge(g["masked"], 9 * (n + 1))
                pe.wait_ge(g["vg_sb"], 2 * (n + 1))
                for h in range(4):
                    v0, v1 = (VG[:, t, h * P:(h + 1) * P] for t in range(2))
                    o = slice(h * P, (h + 1) * P)
                    odd, r = h % 2, h // 2
                    pe.matmul(PB[:, 0, o], SC[:, odd, r, :], v0, start=True, stop=True)
                    pe.matmul(PB[:, 1, o], SC[:, 2, 2 * odd + r, :], v0, start=True, stop=False)
                    last = pe.matmul(PB[:, 1, o], SC[:, odd, 2 + r, :], v1, start=False, stop=True)
                last.then_inc(g["o"], 1)
                pe.wait_ge(g["og"], n + 1)
                for t in range(NT):
                    for k in range(4):
                        last = pe.transpose(PB[:, 2 + t, k * P:(k + 1) * P], OG[:, t, k * P:(k + 1) * P], ident)
                    last.then_inc(g["oT"], 1)

                def bu(r):
                    R = 8 * n + r
                    pe.wait_ge(s5b_in[r % 2], 16 * (4 * n + r // 2 + 1))
                    if r >= 2:
                        pe.wait_ge(s["bu_used"], R - 1)
                    for c in range(2):
                        for t in range(2):
                            last = pe.matmul(PA[:, 2 * (r % 2) + c, t * S:(t + 1) * S], SBM[r % 2][:, c, t, :],
                                             UT[:, r // 2, :], start=True, stop=True)
                    last.then_inc(s["bu"], 1)

                bu(0)
                pe.wait_ge(mix_l, MSTART[b] + 2)
                for r in range(8):
                    if r + 1 < 8:
                        bu(r + 1)
                    pe.wait_ge(s["prod"], 8 * n + r + 1)
                    pe.wait_ge(s["prod2"], 8 * n + r + 1)
                    for t in range(2):
                        st = 2 * r + t
                        o = PB[32 * (st % 4):32 * (st % 4) + 32, r // 2, 0:S]
                        for i, c in enumerate((0, 1, 2, 2)):
                            last = pe.matmul(o, CS[:, c, st, :], TURNED[r % 2][i][:, t * S:(t + 1) * S], start=i == 0, stop=i == 3)
                    last.then_inc(s["y"], 1)

                pe.wait_ge(s["yl"], n + 1)
                pe.wait_ge(s["ysum"], 4 * (n + 1))

                def glu(j):
                    def block_(n_, part):
                        wh, wl = (w.rearrange("p (k n) -> p k n", k=4) for w in flat(n_, part))
                        for c in range(2):
                            m = slice(c * P, (c + 1) * P)
                            for k in range(4):
                                last = mm3(PB[:, 2 * j + c, 0:S], (wh[:, k, m], wl[:, k, m]),
                                           (XH[:, k, :], XL[:, k, :]), k == 0, k == 3)
                        return last
                    return block_

                unit(U + 6, [glu(0), None, glu(1)])
                project(b, U + 7)

            def moe(b):
                for t in range(NT):
                    for k in range(KD):
                        last = pe.matmul(PB[:, 2, 8 * t:8 * t + 8], XTF[:, k, t * P:(t + 1) * P], RW[:, k, :],
                                         start=k == 0, stop=k == KD - 1)
                last.then_inc(logits, 1)
                pe.wait_ge(moe_s["chosen"], 1)
                pe.wait_ge(moe_in, 32)
                chosen = rt[1]
                all_ones = ones.broadcast_to([P, P])
                pe.matmul(PB[:, 2, 32:40], EARLIER, chosen[:, 0, :], start=True, stop=True)
                pe.matmul(PB[:, 2, 40:48], EARLIER, chosen[:, 1, :], start=True, stop=False)
                pe.matmul(PB[:, 2, 40:48], all_ones, chosen[:, 0, :], start=False, stop=True)
                pe.matmul(PB[:, 2, 48:56], all_ones, chosen[:, 0, :], start=True, stop=False)
                pe.matmul(PB[:, 2, 48:56], all_ones, chosen[:, 1, :], start=False, stop=True).then_inc(moe_s["ranks"], 1)

                def gather():
                    for k in range(KD):
                        for t in range(NT):
                            last = pe.matmul(PB[:, 2 + k // 4, (k % 4) * P:(k % 4 + 1) * P],
                                             X[:, t, k * P:(k + 1) * P], ONE[:, t], start=t == 0, stop=t == NT - 1)
                    last.then_inc(moe_s["gathered"], 1)

                def scatter():
                    for t in range(NT):
                        for h in range(2):
                            last = pe.matmul(PA[:, 2 * t + h, :], WGT_T[:, t * P:(t + 1) * P],
                                             YS[:, h * 512:(h + 1) * 512], start=True, stop=True)
                    last.then_inc(moe_s["scattered"], 1)

                def slot_gate_up(i, at, xg):
                    n = N0 + i
                    pe.wait_ge(gu_lo, at + (n + 1))
                    for k in range(KD):
                        last = mm3(PB[:, n % 2, 0:2 * P], tuple(x[xg][:, k, :] for x in (XGH, XGL)),
                                   (wh_gu[n % 2][:, :, k, :], wl_gu[n % 2][:, :, k, :]), k == 0, k == KD - 1)
                    last.then_inc(gu_used, 1)

                def h_transpose(i, at):
                    pe.wait_ge(moe_s["hf"], at + (i + 1))
                    pe.transpose(PB[:, 2 + (N0 + i) % 2, 0:P], HF[(N0 + i) % 2][:, 0:P], ident).then_inc(moe_s["hT"], 1)

                def slot_down(i, at, start, stop):
                    n = N0 + i
                    pe.wait_ge(d_lo, at + (n + 1))
                    pe.wait_ge(h_ready, at + (M0 + i + 1))
                    wh, wl = flat(n, 2)
                    for h in range(2):
                        last = mm3(PA[:, h, :], (HH[n % 2][:, 0:P], HL[n % 2][:, 0:P]),
                                   (wh[:, h * 512:(h + 1) * 512], wl[:, h * 512:(h + 1) * 512]), start, stop)
                    last.then_inc(d_used, 1)

                def sparse(e, xg):
                    at = e * NF2
                    slot_gate_up(0, at, xg)
                    pe.wait_ge(moe_s["wT_sb"], e + 2)
                    slot_gate_up(1, at, xg)
                    pe.wait_ge(moe_s["xg_f"], e + 2)
                    h_transpose(0, at)
                    slot_gate_up(2, at, xg)
                    h_transpose(1, at)
                    pe.wait_ge(moe_s["acc"], e + 2)
                    slot_down(0, at, True, False)
                    slot_gate_up(3, at, xg)
                    h_transpose(2, at)
                    slot_down(1, at, False, False)
                    with pe.Fori(0, (NF2 - 4) // 4) as j:
                        for i in range(4, 8):
                            slot_gate_up(i, at + j * 4, xg)
                            h_transpose(i - 1, at + j * 4)
                            slot_down(i - 2, at + j * 4, False, False)
                    h_transpose(NF2 - 1, at)
                    slot_down(NF2 - 2, at, False, False)
                    slot_down(NF2 - 1, at, False, True)

                def wide_gate_up(i, at):
                    n = N0 + i
                    pe.wait_ge(gu_lo, at + (n + 1))
                    gu_block(n, 0, PB[:, n % 2, 0:S], XH, XL).then_inc(moe_s["hT"], 1)
                    gu_block(n, 1, PB[:, n % 2, S:2 * S], XH, XL).then_inc(gu_used, 1)

                def wide_down(i, at, start, stop):
                    n = N0 + i
                    pe.wait_ge(d_lo, at + (n + 1))
                    pe.wait_ge(h_ready, at + (M0 + i + 1))
                    row_block(n, 2, (HH[n % 2], HL[n % 2]), start, stop).then_inc(d_used, 1)

                def dense(e):
                    at = e * NF2
                    wide_gate_up(0, at)
                    pe.wait_ge(moe_s["wT_sb"], e + 2)
                    wide_gate_up(1, at)
                    pe.wait_ge(moe_s["acc"], e + 2)
                    wide_down(0, at, True, False)
                    wide_gate_up(2, at)
                    wide_down(1, at, False, False)
                    wide_gate_up(3, at)
                    wide_down(2, at, False, False)
                    with pe.Fori(0, (NF2 - 4) // 4) as j:
                        for i in range(4, 8):
                            wide_gate_up(i, at + j * 4)
                            wide_down(i - 1, at + j * 4, False, False)
                    wide_down(NF2 - 1, at, False, True)

                pe.wait_ge(moe_s["onehots"], 1)
                gather()
                with pe.Fori(0, NE // 2) as pair:
                    for r in range(2):
                        e = pair * 2 + r
                        pe.wait_ge(moe_s["onehots"], e + 2)
                        for t in range(NT):
                            last = pe.transpose(PB[:, (N0 + 1) % 2, (2 + t) * P:(3 + t) * P], WGT[:, t], ident)
                        last.then_inc(moe_s["wT"], 1)
                        pe.wait_ge(moe_s["xg_l"], e + 1)
                        gather()
                        pe.wait_ge(moe_s["y"], e + 1)
                        pe.wait_ge(moe_s["wT_sb"], e + 1)
                        scatter()
                        count = pe.value_load(members[:, bass.ds(e, 1)], min_val=0, max_val=S)
                        with pe.If(count <= P):
                            sparse(e, r)
                        with pe.Else():
                            dense(e)
                gate_rows(b)
                pe.wait_ge(moe_s["y"], NE + 1)
                pe.wait_ge(moe_s["wT_sb"], NE + 1)
                scatter()

            for b, (kind, nf) in enumerate(SUBS):
                pre(b)
                if b == len(SUBS) - 1:
                    pe.wait_ge(router_in, 48)
                if kind == "ffn":
                    ffn(START[b], 0, nf, FSTART[b], 0)
                elif kind == "ab":
                    ab(b)
                elif kind == "c":
                    cmix(b)
                elif kind == "mix2":
                    mix2(b)
                else:
                    moe(b)


def kernel(**inputs):
    import concourse.bacc as bacc
    from concourse.bass_utils import run_bass_kernel_spmd

    I = {k: np.asarray(v) for k, v in inputs.items()}
    w_gu = np.zeros((NU, P, 2, BLK), np.float32)
    w_d = np.zeros((NU, P, BLK), np.float32)

    def put(n, part, block):
        if part == 2:
            w_d[n] = block
        else:
            w_gu[n, :, part] = block

    def tcol(w, j):
        c = w[:, j * P:(j + 1) * P]
        if c.shape[1] < P:
            c = np.pad(c, ((0, 0), (0, P - c.shape[1])))
        return c.reshape(KD, P, P).transpose(1, 0, 2).reshape(P, BLK)

    def wide(w, i):
        return w[2 * i * P:(2 * i + 2) * P].reshape(2, P, 512).transpose(1, 0, 2).reshape(P, BLK)

    def rows(w, k):
        return w[k * P:(k + 1) * P]

    def put_ffn(n, wg, wu, wd):
        for f in range(wg.shape[1] // P):
            put(n + f, 0, tcol(wg, f))
            put(n + f, 1, tcol(wu, f))
            put(n + f, 2, rows(wd, f))

    def put_list(n, blocks):
        for i, blk in enumerate(blocks):
            if blk is not None:
                put(n + i // 3, i % 3, blk)

    w_mod = I["mod_w_2"].reshape(2, KD, P, 6, BLK).transpose(0, 3, 1, 2, 4).reshape(96, P, BLK)
    for b, l, name in ((0, 0, "ffn1"), (2, 0, "ffn2"), (3, 1, "ffn1"), (5, 1, "ffn2")):
        put_ffn(START[b], I[name + "_w_gate"][l], I[name + "_w_up"][l], I[name + "_w_down"][l])
    w, o = I["ab_w_in"][0], I["ab_w_out"][0]
    v = w[:, 1024:1536]
    out3 = lambda o: [rows(o, k) for k in range(7)] + [None, rows(o, 7)]
    put_list(START[1], [tcol(w, j) for j in range(8)] + [wide(v, i) for i in range(4)]
             + [tcol(w, j) for j in range(12, 19)] + [None, tcol(w, 19)] + out3(o))
    w = I["c_w_in"][0]
    put_list(START[4], [tcol(w, 8 * i + j) for j in range(8) for i in range(3)] + out3(I["c_w_out"][0]))
    for l, b in ((0, 6), (1, 8)):
        w, glu = I["w_in_2"][l], I["s5_w_glu_2"][l]
        u, q, k, v, go, al = np.split(w, [512, 768, 1024, 1536, 2048], axis=1)
        gb = [glu[:, 256 * j:256 * j + 256].reshape(4, P, 256).transpose(1, 0, 2).reshape(P, BLK) for j in range(2)]
        put_list(START[b], [tcol(q, 0), tcol(q, 1), tcol(k, 0), tcol(k, 1), tcol(al, 0)]
                 + [wide(v, i) for i in range(4)] + [wide(go, i) for i in range(4)]
                 + [tcol(u, 0), tcol(u, 1), tcol(u, 2), None, tcol(u, 3), gb[0], None, gb[1]] + out3(I["w_out_2"][l]))
    put_ffn(START[7], I["ffn_w_gate_2"][0], I["ffn_w_up_2"][0], I["ffn_w_down_2"][0])
    for e in range(NE):
        put_ffn(START[9] + e * NF2, I["moe_w_gate_2"][0, e], I["moe_w_up_2"][0, e], I["moe_w_down_2"][0, e])

    def cols(x):
        return np.asarray(x, np.float32).reshape(-1, P).T

    parts = {
        "c": cols(I["c_2"][0]), "norm_pre": cols(I["norm_pre"]), "conv_w": cols(I["lru_conv_w"][0]),
        "conv_b": cols(I["lru_conv_b"][0]), "ga_b": cols(I["lru_gate_a_b"]), "gx_b": cols(I["lru_gate_x_b"]),
        "lam": cols(I["lru_lambda"][0]), "c_conv": cols(I["c_conv_w"][0]), "mod_b": cols(I["mod_b_2"]),
        "s5_d": cols(I["s5_d_2"]), "glu_b": cols(I["s5_b_glu_2"]), "alpha_b": cols(I["gla_b_alpha_2"]),
        "re": cols(I["s5_lam_re_2"]), "im": cols(I["s5_lam_im_2"]),
        "ldt": cols(np.repeat(I["s5_log_dt_2"].reshape(-1), 64)),
    }
    col = np.concatenate([parts[n] for n in COLS], axis=1)
    assert col.shape == (P, NCOL)

    half = 8
    inv = 500000.0 ** (-np.arange(0, 16, 2, dtype=np.float32) / np.float32(16))
    ang = np.arange(S, dtype=np.float32)[:, None] * inv.astype(np.float32)[None, :]
    cos, sin, rot = np.ones((P, S), np.float32), np.zeros((P, S), np.float32), np.zeros((P, P), np.float32)
    for base in (0, HD):
        for i in range(half):
            cos[base + i] = cos[base + half + i] = np.cos(ang[:, i])
            sin[base + i] = sin[base + half + i] = np.sin(ang[:, i])
            rot[base + half + i, base + i] = -1.0
            rot[base + i, base + half + i] = 1.0
    i, j = np.arange(P)[:, None], np.arange(P)[None, :]
    neg = np.where(j > i, np.float32(-1e30), np.float32(0))
    amask = np.concatenate([neg, np.zeros((P, P), np.float32), neg], axis=1)
    key, query = i, j
    lm = [((key // (2 * w) == query // (2 * w)) & (key % (2 * w) < w) & (query % (2 * w) >= w)) for w in LEVELS]
    tables = {"ident": np.eye(P), "amask": amask, "cos": cos, "sin": sin, "rot": rot,
              "lmask": np.concatenate(lm, axis=1)}
    consts = np.concatenate([tables[n].astype(np.float32) for n in CONST], axis=1)
    assert consts.shape == (P, NCONST)

    gates = np.zeros((P, 2, 4, P), np.float32)
    for gi, name in enumerate(("lru_gate_a_w", "lru_gate_x_w")):
        for h in range(8):
            r = slice(64 * (h % 2), 64 * (h % 2) + 64)
            gates[r, gi, h // 2, r] = I[name][0, h]
    s5_b = np.zeros((2, 8, P, 2, 2, P), np.float32)
    s5_c = np.zeros((2, P, 2, 16, 32), np.float32)
    for l in range(2):
        for c, (nb, ncm) in enumerate((("s5_b_re_2", "s5_c_re_2"), ("s5_b_im_2", "s5_c_im_2"))):
            for gr in range(32):
                st, half_ = gr // 2, gr % 2
                ch = 16 * gr % P
                s5_b[l, st // 2, ch:ch + 16, c, st % 2, 64 * half_:64 * half_ + 64] = I[nb][l, gr].T
                s5_c[l, 64 * half_:64 * half_ + 64, c, st, 16 * half_:16 * half_ + 16] = I[ncm][l, gr].T
    arrays = {
        "w_gu": w_gu.reshape(NU, P, 2 * BLK), "w_d": w_d, "w_mod": w_mod, "cols": np.ascontiguousarray(col), "consts": consts,
        "x": I["x"][0], "norm_post": I["norm_post"].reshape(6, D), "lru_gates": gates,
        "head_gain": I["gla_head_gain_2"], "w_alpha": I["gla_w_alpha_up_2"], "s5_b": s5_b, "s5_c": s5_c,
        "ln_g": np.stack([I["ln_mix_g_2"], I["ln_ffn_g_2"]], 1).reshape(4, D),
        "ln_b": np.stack([I["ln_mix_b_2"], I["ln_ffn_b_2"]], 1).reshape(4, D),
        "router_w": I["moe_w_router_2"][0].reshape(KD, P, NE).transpose(1, 0, 2).copy(),
        "router_b": np.ascontiguousarray(np.broadcast_to(I["moe_b_router_2"][0], (P, 2, NE))),
        "earlier": np.triu(np.ones((P, P), np.float32), 1),
        "slot": np.ascontiguousarray(np.broadcast_to(np.arange(P, dtype=np.float32), (P, P))),
        "first": np.ascontiguousarray(np.broadcast_to(np.arange(NE, 0, -1, dtype=np.float32), (P, 2, NE))),
    }
    arrays = {n: np.ascontiguousarray(x) for n, x in arrays.items()}
    nc = bacc.Bacc("TRN2", target_bir_lowering=False, num_devices=1)
    aps = {n: nc.dram_tensor("in_" + n, x.shape, mybir.dt.from_np(x.dtype), kind="ExternalInput").ap()
           for n, x in arrays.items()}
    out = nc.dram_tensor("out", (S, D), F32, kind="ExternalOutput").ap()
    program(nc, aps, out)
    r = run_bass_kernel_spmd(nc, [{"in_" + n: x for n, x in arrays.items()}], core_ids=[0])
    return r.results[0]["out"].reshape(1, S, D)
```
